# Optimizing a Trainium2 kernel written in Bass

```python
import math
import jax, jax.numpy as jnp
from jax import lax
import numpy as np

D_MODEL = 1024
BATCH = 1
SEQ = 512
DEPTH = 2
DEC_BATCH = 8
DEC_SEQ = 4
PAST_LEN = 1024
PAGE_SIZE = 128

HA_HEADS = 4
HA_DK = 128
HA_DV = 128
HB_HEADS = 8
HB_DIM = 64
HC_HEADS = 4
HC_DK = 128
HC_DV = 128
CONV_W = 4
PEER_HEADS = 8
PEER_TOPK = 16
N_KEYS = 128
N_EXPERTS = N_KEYS * N_KEYS
PEER_QDIM = 256
LIN_CHUNK = 64
Q_BLOCK = 128
PEER_BLOCK = 128
EPS = 1e-6

A_W = HA_HEADS * HA_DK
A_V = HA_HEADS * HA_DV
B_W = HB_HEADS * HB_DIM
C_K = HC_HEADS * HC_DK
C_V = HC_HEADS * HC_DV
CONV_CH = 2 * C_K + C_V
IN_WIDTH = 2 * A_W + 2 * A_V + 3 * B_W + HB_HEADS + 2 * C_K + 2 * C_V + 2 * HC_HEADS + 3 * D_MODEL

kernel_name = "hybrid_hgrn2_fox_gdn_peer_adaln_step"

def _rms(x, g):
    xf = x.astype(jnp.float32)
    r = lax.rsqrt(jnp.mean(xf * xf, axis=-1, keepdims=True) + EPS)
    return (xf * r).astype(x.dtype) * g

def _l2n(x):
    return x * lax.rsqrt(jnp.sum(x * x, axis=-1, keepdims=True) + EPS)

def _heads(t, h):
    return t.reshape(t.shape[0], t.shape[1], h, -1)

def _split_cols(z):
    widths = (A_W, A_W, A_V, A_V, B_W, B_W, B_W, HB_HEADS,
              C_K, C_K, C_V, HC_HEADS, HC_HEADS, C_V, D_MODEL, D_MODEL, D_MODEL)
    out = []
    start = 0
    for w in widths:
        out.append(z[..., start:start + w])
        start += w
    return out

def _hgrn_lower_bounds(logits):
    cs = jnp.cumsum(jax.nn.softmax(logits.astype(jnp.float32), axis=0), axis=0)
    return jnp.maximum(cs - cs[0:1], 0.0)

def _hgrn2_chunked(q, logf, k, v, s0):
    b, L, h, dk = q.shape
    dv = v.shape[-1]
    C = LIN_CHUNK if L % LIN_CHUNK == 0 else L
    n = L // C

    def to_chunks(t):
        return t.reshape(b, n, C, h, t.shape[-1]).transpose(1, 0, 3, 2, 4)

    causal = jnp.tril(jnp.ones((C, C), dtype=bool))

    def step(S, inp):
        qc, gc, kc, vc = inp
        A = jnp.cumsum(gc, axis=2)
        o_inter = jnp.einsum("bhtk,bhkv->bhtv", qc * jnp.exp(A), S)
        rel = A[:, :, :, None, :] - A[:, :, None, :, :]
        dec = jnp.exp(jnp.where(causal[:, :, None], rel, -jnp.inf))
        att = jnp.einsum("bhtk,bhtsk,bhsk->bhts", qc, dec, kc)
        o = o_inter + jnp.einsum("bhts,bhsv->bhtv", att, vc)
        a_last = A[:, :, -1]
        S_new = jnp.exp(a_last)[..., None] * S + jnp.einsum(
            "bhsk,bhsv->bhkv", kc * jnp.exp(a_last[:, :, None, :] - A), vc)
        return S_new, o

    S_fin, o = lax.scan(step, s0.astype(jnp.float32),
                        (to_chunks(q), to_chunks(logf), to_chunks(k), to_chunks(v)))
    return o.transpose(1, 0, 3, 2, 4).reshape(b, L, h, dv), S_fin

def _gdn_chunked(q, k, v, g, beta, s0):
    b, L, h, dk = q.shape
    dv = v.shape[-1]
    C = LIN_CHUNK if L % LIN_CHUNK == 0 else L
    n = L // C

    def chunks4(t):
        return t.reshape(b, n, C, h, t.shape[-1]).transpose(1, 0, 3, 2, 4)

    def chunks3(t):
        return t.reshape(b, n, C, h).transpose(1, 0, 3, 2)

    causal = jnp.tril(jnp.ones((C, C), dtype=bool))
    strict = jnp.tril(jnp.ones((C, C), dtype=bool), -1)
    eye = jnp.eye(C, dtype=jnp.float32)

    def step(S, inp):
        qc, kc, vc, gc, bc = inp
        G = jnp.cumsum(gc, axis=-1)
        rel = G[..., :, None] - G[..., None, :]
        d_strict = jnp.exp(jnp.where(strict, rel, -jnp.inf))
        d_causal = jnp.exp(jnp.where(causal, rel, -jnp.inf))
        eG = jnp.exp(G)[..., None]
        lmat = bc[..., None] * jnp.einsum("bhtk,bhsk->bhts", kc, kc) * d_strict
        rhs = bc[..., None] * (vc - eG * jnp.einsum("bhtk,bhkv->bhtv", kc, S))
        u = lax.linalg.triangular_solve(eye + lmat, rhs, left_side=True, lower=True)
        qk = jnp.einsum("bhtk,bhsk->bhts", qc, kc) * d_causal
        o = eG * jnp.einsum("bhtk,bhkv->bhtv", qc, S) + jnp.einsum("bhts,bhsv->bhtv", qk, u)
        g_last = G[..., -1:]
        S_new = jnp.exp(g_last)[..., None] * S + jnp.einsum(
            "bhsk,bhsv->bhkv", kc * jnp.exp(g_last - G)[..., None], u)
        return S_new, o

    S_fin, o = lax.scan(step, s0.astype(jnp.float32),
                        (chunks4(q), chunks4(k), chunks4(v), chunks3(g), chunks3(beta)))
    return o.transpose(1, 0, 3, 2, 4).reshape(b, L, h, dv), S_fin

def _causal_conv(x, buf, w):
    xp = jnp.concatenate([buf.astype(x.dtype), x], axis=1)
    L = x.shape[1]
    y = xp[:, 0:L] * w[0]
    for j in range(1, CONV_W):
        y = y + xp[:, j:j + L] * w[j]
    return jax.nn.silu(y), xp[:, -(CONV_W - 1):]

def _fox_attend(q, Fq, pos_q, k, v, Fk, pos_k):
    s = jnp.einsum("bthd,bshd->bhts", q, k).astype(jnp.float32) * (HB_DIM ** -0.5)
    s = s + (Fq[..., :, None] - Fk[..., None, :])
    s = jnp.where(pos_k[None, :] <= pos_q[:, None], s, -jnp.inf)
    p = jax.nn.softmax(s, axis=-1)
    return jnp.einsum("bhts,bshd->bthd", p.astype(v.dtype), v)

def _fox_prompt(q, k, v, logf):
    b, S, h, d = q.shape
    F = jnp.cumsum(logf, axis=1).transpose(0, 2, 1)
    nb = S // Q_BLOCK
    pos_k = jnp.arange(S)
    qb = q.reshape(b, nb, Q_BLOCK, h, d).transpose(1, 0, 2, 3, 4)
    Fb = F.reshape(b, h, nb, Q_BLOCK).transpose(2, 0, 1, 3)

    def blk(args):
        i, qi, Fi = args
        return _fox_attend(qi, Fi, i * Q_BLOCK + jnp.arange(Q_BLOCK), k, v, F, pos_k)

    o = lax.map(blk, (jnp.arange(nb), qb, Fb))
    return o.transpose(1, 0, 2, 3, 4).reshape(b, S, h * d)

def _fox_sample(q, k, v, logf, k_past, v_past, logf_past):
    b, T, h, d = q.shape
    P = k_past.shape[1]
    kk = jnp.concatenate([k_past.astype(k.dtype), k], axis=1)
    vv = jnp.concatenate([v_past.astype(v.dtype), v], axis=1)
    lf = jnp.concatenate([logf_past.astype(jnp.float32), logf], axis=1)
    F = jnp.cumsum(lf, axis=1).transpose(0, 2, 1)
    o = _fox_attend(q, F[..., P:], P + jnp.arange(T), kk, vv, F, jnp.arange(P + T))
    return o.reshape(b, T, h * d)

def _mixers(l, h, p, lb, fox_fn, s_hgrn, s_gdn, conv_buf):
    b, L, _ = h.shape
    f32 = jnp.float32
    z = h @ p["w_in"][l]
    (fa, qa, ia, ga, qb, kb, vb, fb, qc, kc, vc, ac, bc, zc,
     gate_a, gate_b, gate_c) = _split_cols(z)

    lb_h = lb.reshape(HA_HEADS, HA_DK)
    log_f = jnp.logaddexp(jnp.log(lb_h), jnp.log1p(-lb_h) + jax.nn.log_sigmoid(_heads(fa, HA_HEADS).astype(f32)))
    k_in = -jnp.expm1(log_f)
    o_a, s_hgrn_new = _hgrn2_chunked(jax.nn.silu(_heads(qa, HA_HEADS).astype(f32)), log_f, k_in,
                                     _heads(ia, HA_HEADS).astype(f32), s_hgrn)
    o_a = _rms(o_a, p["hgrn_norm"][l]) * jax.nn.silu(_heads(ga, HA_HEADS).astype(f32))
    y_a = o_a.reshape(b, L, A_V).astype(h.dtype) @ p["w_br_a"][l]

    q_b = _rms(_heads(qb, HB_HEADS), p["fox_q_norm"][l])
    k_b = _rms(_heads(kb, HB_HEADS), p["fox_k_norm"][l])
    v_b = _heads(vb, HB_HEADS)
    logf_b = jax.nn.log_sigmoid((fb + p["fox_b_f"][l]).astype(f32))
    y_b = fox_fn(l, q_b, k_b, v_b, logf_b) @ p["w_br_b"][l]

    qkv, conv_new = _causal_conv(jnp.concatenate([qc, kc, vc], axis=-1), conv_buf, p["gdn_conv_w"][l])
    q_c = _l2n(_heads(qkv[..., :C_K], HC_HEADS).astype(f32)) * (HC_DK ** -0.5)
    k_c = _l2n(_heads(qkv[..., C_K:2 * C_K], HC_HEADS).astype(f32))
    v_c = _heads(qkv[..., 2 * C_K:], HC_HEADS).astype(f32)
    g_c = -jnp.exp(p["gdn_a_log"][l].astype(f32)) * jax.nn.softplus((ac + p["gdn_dt_bias"][l]).astype(f32))
    beta = jax.nn.sigmoid(bc.astype(f32))
    o_c, s_gdn_new = _gdn_chunked(q_c, k_c, v_c, g_c, beta, s_gdn)
    o_c = _rms(o_c, p["gdn_norm"][l]) * jax.nn.silu(_heads(zc, HC_HEADS).astype(f32))
    y_c = o_c.reshape(b, L, C_V).astype(h.dtype) @ p["w_br_c"][l]

    merged = jax.nn.sigmoid(gate_a) * y_a + jax.nn.sigmoid(gate_b) * y_b + jax.nn.sigmoid(gate_c) * y_c
    return merged @ p["w_out"][l], (k_b, v_b, logf_b, s_hgrn_new, s_gdn_new, conv_new)

def _peer(x, w_q, keys, u_tab, v_tab):
    t_all = x.shape[0]
    blk = PEER_BLOCK if t_all % PEER_BLOCK == 0 else t_all

    def run(xb):
        q = (xb @ w_q).reshape(blk, PEER_HEADS, 2, PEER_QDIM // 2)
        s = jnp.einsum("thpd,pnd->thpn", q, keys).astype(jnp.float32)
        sv, si = lax.top_k(s, PEER_TOPK)
        cand = sv[:, :, 0, :, None] + sv[:, :, 1, None, :]
        cidx = si[:, :, 0, :, None] * N_KEYS + si[:, :, 1, None, :]
        best, pos = lax.top_k(cand.reshape(blk, PEER_HEADS, PEER_TOPK * PEER_TOPK), PEER_TOPK)
        eidx = jnp.take_along_axis(cidx.reshape(blk, PEER_HEADS, PEER_TOPK * PEER_TOPK), pos, axis=-1)
        g = jax.nn.softmax(best, axis=-1)
        act = jax.nn.gelu(jnp.einsum("thkd,td->thk", u_tab[eidx], xb).astype(jnp.float32))
        return jnp.einsum("thk,thkd->td", (g * act).astype(xb.dtype), v_tab[eidx])

    y = lax.map(run, x.reshape(t_all // blk, blk, D_MODEL))
    return y.reshape(t_all, D_MODEL)

def _trunk(x, c, fox_fn, s_hgrn, s_gdn, s_conv, p):
    b, L, _ = x.shape
    lbs = _hgrn_lower_bounds(p["hgrn_lb_logits"])
    outs = [[] for _ in range(6)]
    for l in range(DEPTH):
        mod = (jax.nn.silu(c) @ p["w_ada"][l] + p["b_ada"][l])[:, None, :]
        sh1, sc1, gt1, sh2, sc2, gt2 = jnp.split(mod, 6, axis=-1)
        h = _rms(x, p["norm_mix"][l]) * (1.0 + sc1) + sh1
        mix, st = _mixers(l, h, p, lbs[l], fox_fn, s_hgrn[l], s_gdn[l], s_conv[l])
        x = x + gt1 * mix
        h2 = _rms(x, p["norm_ffn"][l]) * (1.0 + sc2) + sh2
        ffn = _peer(h2.reshape(b * L, D_MODEL), p["peer_w_q"][l], p["peer_keys"][l],
                    p["peer_u"][l], p["peer_v"][l])
        x = x + gt2 * ffn.reshape(b, L, D_MODEL)
        for lst, s in zip(outs, st):
            lst.append(s)
    return x, [jnp.stack(o) for o in outs]

def setup_inputs(seed: int = 0) -> dict:
    key = jax.random.key(seed)
    k = jax.random.split(key, 32)
    f32 = jnp.float32
    n_pages = PAST_LEN // PAGE_SIZE
    used = DEC_BATCH * n_pages
    n_pool = used + max(1, used // 4)

    def nrm(i, shape, scale=1.0):
        return jax.random.normal(k[i], shape, f32) * scale

    def gain(i, shape):
        return 1.0 + 0.05 * jax.random.normal(k[i], shape, f32)

    dt = jnp.exp(jax.random.uniform(k[24], (DEPTH, HC_HEADS), f32, math.log(1e-3), math.log(1e-1)))
    return {
        "x_prompt": nrm(0, (BATCH, SEQ, D_MODEL)),
        "x_sample": nrm(1, (DEC_BATCH, DEC_SEQ, D_MODEL)),
        "c_prompt": nrm(2, (BATCH, D_MODEL)),
        "c_sample": nrm(3, (DEC_BATCH, D_MODEL)),
        "cache_fox_k": nrm(4, (DEPTH, n_pool, PAGE_SIZE, HB_HEADS, HB_DIM)),
        "cache_fox_v": nrm(5, (DEPTH, n_pool, PAGE_SIZE, HB_HEADS, HB_DIM)),
        "cache_fox_logf": jax.nn.log_sigmoid(4.0 + 0.5 * jax.random.normal(k[6], (DEPTH, n_pool, PAGE_SIZE, HB_HEADS), f32)),
        "page_table": jax.random.permutation(k[7], n_pool)[:used].reshape(DEC_BATCH, n_pages).astype(jnp.int32),
        "state_hgrn": nrm(8, (DEPTH, DEC_BATCH, HA_HEADS, HA_DK, HA_DV), 0.5),
        "state_gdn": nrm(9, (DEPTH, DEC_BATCH, HC_HEADS, HC_DK, HC_DV), 0.1),
        "state_gdn_conv": nrm(10, (DEPTH, DEC_BATCH, CONV_W - 1, CONV_CH)),
        "w_ada": nrm(11, (DEPTH, D_MODEL, 6 * D_MODEL), 0.2 * D_MODEL ** -0.5),
        "b_ada": nrm(12, (DEPTH, 6 * D_MODEL), 0.02),
        "norm_mix": gain(13, (DEPTH, D_MODEL)),
        "norm_ffn": gain(14, (DEPTH, D_MODEL)),
        "w_in": nrm(15, (DEPTH, D_MODEL, IN_WIDTH), D_MODEL ** -0.5),
        "hgrn_lb_logits": nrm(16, (DEPTH, A_W), 0.5),
        "hgrn_norm": gain(17, (DEPTH, HA_DV)),
        "fox_b_f": 3.0 + nrm(18, (DEPTH, HB_HEADS), 0.5),
        "fox_q_norm": gain(19, (DEPTH, HB_DIM)),
        "fox_k_norm": gain(20, (DEPTH, HB_DIM)),
        "gdn_conv_w": nrm(21, (DEPTH, CONV_W, CONV_CH), CONV_W ** -0.5),
        "gdn_a_log": jnp.log(jax.random.uniform(k[22], (DEPTH, HC_HEADS), f32, 1.0, 16.0)),
        "gdn_dt_bias": dt + jnp.log(-jnp.expm1(-dt)),
        "gdn_norm": gain(23, (DEPTH, HC_DV)),
        "w_br_a": nrm(25, (DEPTH, A_V, D_MODEL), A_V ** -0.5),
        "w_br_b": nrm(26, (DEPTH, B_W, D_MODEL), B_W ** -0.5),
        "w_br_c": nrm(27, (DEPTH, C_V, D_MODEL), C_V ** -0.5),
        "w_out": nrm(28, (DEPTH, D_MODEL, D_MODEL), D_MODEL ** -0.5),
        "peer_w_q": nrm(29, (DEPTH, D_MODEL, PEER_HEADS * PEER_QDIM), D_MODEL ** -0.5),
        "peer_keys": nrm(30, (DEPTH, 2, N_KEYS, PEER_QDIM // 2), (PEER_QDIM // 2) ** -0.5),
        "peer_u": nrm(31, (DEPTH, N_EXPERTS, D_MODEL), D_MODEL ** -0.5),
        "peer_v": jax.random.normal(jax.random.fold_in(key, 99), (DEPTH, N_EXPERTS, D_MODEL), f32),
    }

def reference(x_prompt, x_sample, c_prompt, c_sample, cache_fox_k, cache_fox_v, cache_fox_logf, page_table,
              state_hgrn, state_gdn, state_gdn_conv, w_ada, b_ada, norm_mix, norm_ffn, w_in, hgrn_lb_logits,
              hgrn_norm, fox_b_f, fox_q_norm, fox_k_norm, gdn_conv_w, gdn_a_log, gdn_dt_bias, gdn_norm,
              w_br_a, w_br_b, w_br_c, w_out, peer_w_q, peer_keys, peer_u, peer_v):
    p = {"w_ada": w_ada, "b_ada": b_ada, "norm_mix": norm_mix, "norm_ffn": norm_ffn, "w_in": w_in,
         "hgrn_lb_logits": hgrn_lb_logits, "hgrn_norm": hgrn_norm, "fox_b_f": fox_b_f,
         "fox_q_norm": fox_q_norm, "fox_k_norm": fox_k_norm, "gdn_conv_w": gdn_conv_w,
         "gdn_a_log": gdn_a_log, "gdn_dt_bias": gdn_dt_bias, "gdn_norm": gdn_norm,
         "w_br_a": w_br_a, "w_br_b": w_br_b, "w_br_c": w_br_c, "w_out": w_out,
         "peer_w_q": peer_w_q, "peer_keys": peer_keys, "peer_u": peer_u, "peer_v": peer_v}
    bp = x_prompt.shape[0]
    db, n_pages = page_table.shape

    hgrn0 = jnp.zeros((DEPTH, bp, HA_HEADS, HA_DK, HA_DV), jnp.float32)
    gdn0 = jnp.zeros((DEPTH, bp, HC_HEADS, HC_DK, HC_DV), jnp.float32)
    conv0 = jnp.zeros((DEPTH, bp, CONV_W - 1, CONV_CH), x_prompt.dtype)

    def fox_prompt_fn(l, q, k, v, lf):
        return _fox_prompt(q, k, v, lf)

    def fox_sample_fn(l, q, k, v, lf):
        kp = cache_fox_k[l][page_table].reshape(db, n_pages * PAGE_SIZE, HB_HEADS, HB_DIM)
        vp = cache_fox_v[l][page_table].reshape(db, n_pages * PAGE_SIZE, HB_HEADS, HB_DIM)
        lp = cache_fox_logf[l][page_table].reshape(db, n_pages * PAGE_SIZE, HB_HEADS)
        return _fox_sample(q, k, v, lf, kp, vp, lp)

    y_prompt, (fox_k_p, fox_v_p, fox_lf_p, hgrn_p, gdn_p, conv_p) = _trunk(
        x_prompt, c_prompt, fox_prompt_fn, hgrn0, gdn0, conv0, p)
    y_sample, (fox_k_s, fox_v_s, fox_lf_s, hgrn_s, gdn_s, conv_s) = _trunk(
        x_sample, c_sample, fox_sample_fn, state_hgrn, state_gdn, state_gdn_conv, p)
    return (y_prompt, y_sample, fox_k_p, fox_v_p, fox_lf_p, hgrn_p, gdn_p, conv_p,
            fox_k_s, fox_v_s, fox_lf_s, hgrn_s, gdn_s, conv_s)


_drawn_inputs = setup_inputs


def setup_inputs(seed=0):
    import zlib

    import numpy as np

    out = dict(_drawn_inputs(seed))
    spreads = {}
    factors = {'cache_fox_k': 4.259,
     'cache_fox_v': 3.256,
     'cache_fox_logf': 8.0,
     'hgrn_norm': 8.0,
     'fox_q_norm': 8.0,
     'gdn_norm': 8.0}
    for name, (base, spread) in spreads.items():
        noise = np.random.default_rng([zlib.crc32(name.encode()), seed]).standard_normal(out[name].shape)
        drawn = base * np.exp(spread * noise) if base else spread * noise
        out[name] = __import__('jax').numpy.asarray(drawn.astype(out[name].dtype))
    for name, factor in factors.items():
        out[name] = (out[name] * factor).astype(out[name].dtype)
    return out
```

```python
import numpy as np
import concourse.bass as bass
from concourse import mybir

ALU = mybir.AluOpType
ACT = mybir.ActivationFunctionType
F32 = mybir.dt.float32
U32 = mybir.dt.uint32
I32 = mybir.dt.int32
AX = mybir.AxisListType

P = 128
DM = 1024
DC = DM // P
L = 2
TP, NSEQ, TS = 512, 8, 4
TSA = NSEQ * TS
T = TP + TSA
HT = T // 2
NT = TP // P
H = 4
HB = 8
PAST, PAGE = 1024, 128
NPG = PAST // PAGE
EPS = 1e-6
NK = 128
KT = 16
JS = 2
NEG = -1e30
LOWEST = -3.0e38

S_F, S_K, S_Q, S_GA, S_ZC, S_I, S_QC, S_KC, S_VC, S_QB, S_KB, S_VB = (4 * i for i in range(12))
S_MG, S_QP, S_XSQ, S_SC, S_CD = 12, 12, 28, 36, 40
NSLOT = 48
RING = 4
G_ADA, G_Z, G_MG, G_OUT, G_Q = 12, 11, 10, 2, 4
B_Z = G_ADA
B_MG = B_Z + G_Z
B_OUT = B_MG + G_MG
B_Q = B_OUT + G_OUT
G_W = B_Q + G_Q
G_U, G_V = 32, 32
G_ALL = G_W + 2 * (G_U + G_V)
CN = {}
_o = 0
for _n, _w in (("sel1", 39), ("selP", 15), ("selq", 38), ("selk", 38), ("hb2", 1), ("hb3", 1), ("lm", 7 * 128), ("strict", 128), ("causal", 128), ("blk16", 128), ("neg", 128),
               ("strict4", 32), ("causal4", 32), ("ms", 256), ("sel8", 256), ("smk", 256), ("sm", 8), ("md", 8),
               ("selt", 4), ("sgn", 1), ("nsel", 16)):
    CN[_n] = (_o, _w)
    _o += _w
NCN = _o
PR = {}
_o = 0
for _n, _w in (("b_ada", 48), ("nmix", 8), ("nffn", 8), ("hg", 1), ("qg", 1), ("kg", 1), ("gg", 1), ("conv", 48),
               ("rb", 1), ("al", 1), ("keys", 256)):
    PR[_n] = (_o, _w)
    _o += _w
NPR = _o
C_CN = NSLOT * T
C_W = C_CN + NCN
NTILE = 13
C_SQ = C_W + NTILE * 512
C_GB = P * HT
C_OH = C_GB + 2 * HT
NAR = C_OH + 4 * 512
assert C_SQ + 4 * T <= NAR


def shape_constants():
    s, t = np.arange(P)[:, None], np.arange(P)[None, :]
    x = s ^ t
    c = np.zeros((P, NCN), np.float32)

    def put(name, a):
        o, w = CN[name]
        a = np.asarray(a, np.float32).reshape(a.shape[0], -1)
        assert a.shape[1] == w, name
        c[:a.shape[0], o:o + w] = a

    one = np.ones((P, 1), np.float32)
    pad = lambda n, x: np.pad(x, ((0, 0), (n, n)))
    two = np.stack([np.arange(P) < 64, np.arange(P) >= 64], 1)
    put("sel1", pad(19, one))
    put("selP", pad(7, one * P))
    put("selq", pad(18, two * 128.0))
    put("selk", pad(18, two * 2.0))
    put("hb2", np.where(np.arange(8) < 4, P * EPS, EPS)[:, None])
    put("hb3", np.where((np.arange(20) >= 4) & (np.arange(20) < 12), 64 * EPS, EPS)[:, None])
    put("lm", np.stack([(x >= b) & (x < 2 * b) & (t > s) for b in (1, 2, 4, 8, 16, 32, 64)], 1))
    put("strict", t > s)
    put("causal", t >= s)
    put("blk16", x < 16)
    put("neg", np.where(t > s, NEG, 0.0))
    put("strict4", ((x < 4) & (t > s))[:32, :32])
    put("causal4", ((x < 4) & (t >= s))[:32, :32])
    r = np.arange(32)
    q, k = np.arange(8)[None, :, None], np.arange(32)[None, None, :]
    ok = (k >= 4 * q) & (k <= 4 * q + (r % 4)[:, None, None])
    put("ms", np.where(ok, 0.0, NEG))
    rows = np.arange(64)[:, None, None]
    put("sel8", -1.0 * ((rows // 8 == q) & (rows % 8 == k // 4)))
    put("smk", np.broadcast_to(k // 4 == q, (P, 8, 32)))
    put("sm", r[:, None] // 4 == np.arange(8)[None, :])
    put("md", r[:, None] // 4 == np.arange(8)[None, :])
    put("selt", r[:, None] % 4 == np.arange(4)[None, :])
    sg = np.ones((16, 1)); sg[:8] = -1.0
    put("sgn", sg)
    put("nsel", -np.eye(16))
    return c


def build(nc, a, o):
    sb = lambda name, shape, dt=F32: nc.alloc_sbuf_tensor(name, shape, dt)
    AR = sb("arena", [P, NAR])
    xT = sb("xT", [P, DC, T])
    hT = sb("hT", [P, DC, T])
    ring = sb("ring", [P, RING, DC, P])
    ident = sb("ident", [P, P])
    ones = sb("ones", [P, P])
    iota = sb("iota", [P, P])
    MOD = sb("MOD", [P, 48, 9])
    PRM = sb("PRM", [P, NPR])
    cT = sb("cT", [P, DC, 9])
    LB = sb("LB", [P, L, H])
    LBC = sb("LBC", [P, 2, H])
    RO = sb("RO", [P, 3, T])
    epsc = sb("epsc", [P, 3])
    rs8 = sb("rs8", [P, 2, HB])
    PS = nc.alloc_psum_tensor("PS", [P, 8, 512], F32)

    def slots(i, n):
        return AR[:, i * T:(i + n) * T].rearrange("p (s t) -> p s t", t=T)

    ZALL = slots(0, NSLOT)
    W = [AR[:, C_W + 512 * i:C_W + 512 * (i + 1)] for i in range(NTILE)]
    wide = lambda i, n: AR[:, C_W + 512 * i:C_W + 512 * i + n]
    SQ = [AR[:, C_SQ + T * i:C_SQ + T * (i + 1)] for i in range(4)]
    cn = lambda n: AR[:, C_CN + CN[n][0]:C_CN + CN[n][0] + CN[n][1]]
    pr = lambda n: PRM[:, PR[n][0]:PR[n][0] + PR[n][1]]
    Fs, Ks, Qs, GAs, ZCs, Is = (slots(i, 4) for i in (S_F, S_K, S_Q, S_GA, S_ZC, S_I))
    QCs, KCs, VCs, QBs, KBs, VBs = (slots(i, 4) for i in (S_QC, S_KC, S_VC, S_QB, S_KB, S_VB))
    KBETA, QE = Is, GAs
    RRt = slots(0, 8)
    R_L, R_B, R_G, R_F, R_E, R_D, R_X, R_Y = (RRt[0:16, i, :] for i in range(8))
    ZS = RO[0:16, 0, :]
    XSQ = slots(S_XSQ, 8)
    MG = slots(S_MG, 8)
    QP = slots(S_QP, 16)
    halves = lambda ap: ap.rearrange("p (a b) -> p a b", a=2)
    pair = lambda b: PS[:, b:b + 2, 0:HT]
    WB = AR[:, 0:P * HT].rearrange("p (i t) -> p i t", t=HT)
    WBt = AR[:, 0:P * HT].rearrange("p (i t) -> p t i", t=HT)
    GB = [AR[:, C_GB + HT * i:C_GB + HT * (i + 1)] for i in range(2)]
    OHJ = [AR[:, C_OH + 512 * i:C_OH + 512 * (i + 1)].rearrange("p (t j) -> p t j", t=4) for i in range(2)]
    OHI = [AR[:, C_OH + 1024 + 512 * i:C_OH + 1024 + 512 * (i + 1)].rearrange("p (t j) -> p t j", t=4) for i in range(2)]
    EGL = RO[:, 2, 400:448].rearrange("p (h n) -> p h n", h=H)
    CT = RO[:, 1, 0:400].rearrange("p (n k r) -> p n k r", n=5, k=5)
    nmx = sb("nmx", [P, 2])
    RC = sb("RC", [P, 4])
    rtmp = sb("rtmp", [P, TSA])
    CO = RO[:, 2, 0:324].rearrange("p (n t) -> p n t", n=12)
    iota16 = iota[:, 0:16]
    NTS = [(i * P, P) for i in range(NT)] + [(TP, TSA)]

    init_ld, init_v, init_c = (nc.alloc_semaphore(n) for n in ("init_loads", "init_bounds", "init_silu"))

    class Sig:
        def __init__(self, name, n, first=0):
            self.sem, self.n, self.first, self.name = nc.alloc_semaphore(name), n, first, name
        def at(self, l, k):
            return l * self.n + (k + self.first)

    sem = nc.alloc_semaphore
    ring_full = [sem(f"ring_full{s}") for s in range(RING)]
    ring_used = [sem(f"ring_used{s}") for s in range(RING)]
    prm_ld, tab_ld = Sig("params_loaded", 16), Sig("tables_loaded", 32)
    out_st = Sig("outputs_stored", 16 * 6)
    sq_r, ms_mm, rt_r, h_r = Sig("x_squared", 2), Sig("x_ss", 2), Sig("x_rms", 2), Sig("h_ready", 2)
    zs_mm, zs_r = Sig("small_mm", 1), Sig("small_ready", 1)
    z_ev = Sig("z_ready", 44, 2)
    hg_lvl, att_mm, att_cp = Sig("hgrn_level_ready", 9), Sig("hgrn_att_mm", 35), Sig("hgrn_att_copied", 35, 4)
    hv_mm, hv_cp, ho_mm, ho_cp = Sig("hgrn_tok_mm", 5), Sig("hgrn_tok_ready", 5), Sig("hgrn_out_mm", 4), Sig("hgrn_state_ready", 4)
    ss_ld = [Sig("seq_states_loaded0", 16 * 4), Sig("seq_states_loaded1", 16 * 4)]
    ss_up, ss_st = Sig("seq_states_updated", 8), Sig("seq_states_stored", 16 * 8)
    bd_r, sd_mm, so_mm = Sig("seq_blocks_ready", 8), Sig("seq_state_mm", 8), Sig("seq_out_mm", 2)
    hn_go = Sig("headnorm_input_ready", 2)
    hn_sq, hn_mm, hn_rt = Sig("headnorm_squared", 24), Sig("headnorm_summed", 24), Sig("headnorm_roots", 3)
    hn_rc, hn_sp, hn_ap = Sig("headnorm_scales", 3), Sig("headnorm_spread", 24), Sig("headnorm_applied", 24)

    HN = ([(S_Q + h, "sel1", h, 1, "hg") for h in range(4)],
          [(S_QC + h, "selP", h, 1, None) for h in range(4)] + [(S_KC + h, "sel1", 4 + h, 1, None) for h in range(4)],
          [(S_VC + h, "sel1", h, 1, "gg") for h in range(4)]
          + [(S_QB + c, "selq", 4 + 2 * c, 2, "qg") for c in range(4)] + [(S_KB + c, "selk", 12 + 2 * c, 2, "kg") for c in range(4)])
    HN_BASE, HN_ROWS = (0, 4, 12), (4, 8, 20)
    HN_SCALE = (1.0 / P, 1.0, 1.0 / P)
    oa_r, oc_r, ob_r = Sig("branch_a_ready", 1), Sig("branch_c_ready", 1), Sig("branch_b_ready", 1)
    cv_ld, cv_v, cv_s = Sig("conv_state_loaded", 16), Sig("conv_summed", 13), Sig("conv_ready", 13)
    rw_u, rw_e = Sig("rows_input", 1), Sig("rows_softplus", 1)
    rw_g, rw_x = Sig("rows_cumulated", 1), Sig("rows_exp", 1)
    ct_mm, ct_r = Sig("row_columns_mm", 1), Sig("row_columns_ready", 1)
    bc_mm, bc_v = Sig("row_spread_mm", 8), Sig("row_spread_used", 8)
    g_mm, g_v, g_s = Sig("gdn_mm", 4 * 18 + 16), Sig("gdn_vector", 4 * 18 + 17), Sig("gdn_scalar", 4 * 8 + 7)
    gk_r, gw_r, gu_mm, gu_s = Sig("gdn_kv_ready", 5), Sig("gdn_w_masked", 4), Sig("gdn_seq_u_mm", 4), Sig("gdn_seq_u_ready", 4)
    gq_r = Sig("gdn_inputs_ready", 1)
    fv_mm, fv_cp = Sig("fox_vtok_mm", 5), Sig("fox_vtok_ready", 5)
    fs_mm, fs_nm, fs_ex = Sig("fox_scores_mm", 32), Sig("fox_max_ready", 32), Sig("fox_probs_ready", 32)
    fp_mm, fp_cp, fo_mm = Sig("fox_probs_t_mm", 32), Sig("fox_probs_t_ready", 32), Sig("fox_out_mm", 32)
    fn_r, ft_mm, ft_cp = Sig("fox_out_scaled", 4), Sig("fox_out_t_mm", 4), Sig("fox_out_t_ready", 4)
    fx_r = Sig("fox_qk_ready", 1)
    pt_ld = Sig("page_table_loaded", 16)
    lg_ld, ln_ld, lg_r = Sig("past_logf_loaded", 16 * 64), Sig("new_logf_loaded", 16 * 8), Sig("past_forget_ready", 1)
    kc_ld = [Sig("k_pages_loaded0", 16 * 32), Sig("k_pages_loaded1", 16 * 32)]
    vc_ld = [Sig("v_pages_loaded0", 16 * 32), Sig("v_pages_loaded1", 16 * 32)]
    qs_mm, qs_nm, qs_ex = Sig("seq_scores_mm", 8), Sig("seq_max_ready", 8), Sig("seq_probs_ready", 8)
    qp_mm, qp_cp, qo_mm = Sig("seq_probs_t_mm", 8), Sig("seq_probs_t_ready", 8), Sig("seq_pv_mm", 8)
    qn_r, qt_mm, qt_cp = Sig("seq_heads_picked", 8), Sig("seq_out_t_mm", 8), Sig("seq_out_ready", 8)
    mg_mm, mg_sg, mg_v = Sig("merge_branch_a_mm", 8), Sig("merge_gate", 24), Sig("merged", 24, 2)
    wo_v = Sig("out_added", 8, 2)
    qj_s = Sig("query_ready", 16, 2)
    sc_mm, sc_s = Sig("key_scores_mm", 5), Sig("key_scores_ready", 5)
    tk_v, sx_e, rt_v = Sig("best_centred", 5), Sig("best_exp", 5), Sig("routes_ready", 5)
    rr_mm, rr_s = Sig("routes_t_mm", 5), Sig("routes_t_ready", 5)
    oi_v, oj_s, oh_mm, w_ev = Sig("onehots_ready", 136), Sig("onehots_scalar_ready", 136), Sig("weights_mm", 136, 2), Sig("weights_ready", 136, 2)
    gl_s, a_v = Sig("expert_gelu", 256, 2), Sig("expert_act_ready", 256, 2)
    y_v = Sig("expert_out_added", 16, 2)

    PTAB = RO[0:1, 2, 448:512].bitcast(I32)
    LG = AR[:, 6 * T:6 * T + 1056]
    k_pages = lambda q: AR[:, 12 * T + (q % 2) * 4096:12 * T + (q % 2 + 1) * 4096].rearrange("p (c s) -> p c s", c=4)
    probs1 = lambda q: AR[:, 12 * T + 8192 + (q % 2) * 1056:12 * T + 8192 + (q % 2 + 1) * 1056]

    def v_page(q, pg):
        o_ = C_W + (8 + pg) * 512 if q % 2 == 0 else pg * 512 if pg < 6 else C_W + (5 + pg - 6) * 512
        return AR[:, o_:o_ + 512]

    def tiles_in(l, k):
        return (l * G_ALL + k + 1) * 16

    def tiles_used(l, k):
        return l * G_ALL + k + 1

    block_cm = nc.Block()
    block = block_cm.__enter__()

    @block.sync
    def _(sp):
        with sp.Fori(0, L) as l:
            with sp.Fori(0, B_MG) as k:
                for s in range(RING):
                    sp.wait_ge(ring_used[s], l * G_ALL + k)
                    sp.dma_start(ring[:, s, :, :], a["wst"][(l * G_W + k) * RING + s]).then_inc(ring_full[s], 16)
            sp.wait_ge(pt_ld.sem, pt_ld.at(l, 16))
            sp.nop(nofuse=True)
            sp.wait_ge(oc_r.sem, oc_r.at(l, 1))
            sp.nop(nofuse=True)
            for q in range(NSEQ):
                if q >= 2:
                    sp.wait_ge(qs_mm.sem, qs_mm.at(l, q - 1))
                    sp.nop(nofuse=True)
                for pg in range(NPG):
                    r = sp.value_load(PTAB[0:1, q * NPG + pg:q * NPG + pg + 1], min_val=0, max_val=a["ck"].shape[1] - 1)
                    sp.dma_start(k_pages(q)[:, :, pg * PAGE:(pg + 1) * PAGE], a["ck"][l, r]).then_inc(kc_ld[q % 2].sem, 16)
            with sp.Fori(B_MG, G_W) as k:
                for s in range(RING):
                    sp.wait_ge(ring_used[s], l * G_ALL + k)
                    sp.dma_start(ring[:, s, :, :], a["wst"][(l * G_W + k) * RING + s]).then_inc(ring_full[s], 16)
            with sp.Fori(0, 2) as hf:
                with sp.Fori(0, G_U + G_V) as k:
                    for s in range(RING):
                        sp.wait_ge(ring_used[s], l * G_ALL + (hf * (G_U + G_V) + k + G_W))
                        sp.dma_start(ring[:, s, :, :], a["uv"][(l * (G_U + G_V) + k) * RING + s]).then_inc(ring_full[s], 16)

    @block.gpsimd
    def _(g):
        for dst, src in ((xT[:, :, :], a["x"]), (ident[:, :], a["id"]), (ones[:, :], a["ones"]), (iota[:, :], a["iota"]),
                         (cT[:, :, :], a["c"]), (LB[:, :, :], a["lb"])):
            g.dma_start(dst, src).then_inc(init_ld, 16)
        def seq_states(l, src, dst, base, bufs):
            for h in range(H):
                if h >= 2:
                    g.wait_ge(ss_up.sem, ss_up.at(l, base + h - 1))
                    g.nop(nofuse=True)
                    g.dma_start(dst[l, h - 2], bufs[h % 2]).then_inc(ss_st.sem, 16)
                    g.wait_ge(ss_st.sem, ss_st.at(l, 16 * (base + h - 1)))
                    g.nop(nofuse=True)
                g.dma_start(bufs[h % 2], src[l, h]).then_inc(ss_ld[h % 2].sem, 16)
            for h in (2, 3):
                g.wait_ge(ss_up.sem, ss_up.at(l, base + h + 1))
                g.nop(nofuse=True)
                g.dma_start(dst[l, h], bufs[h % 2]).then_inc(ss_st.sem, 16)
            g.wait_ge(ss_st.sem, ss_st.at(l, 16 * (base + 4)))
            g.nop(nofuse=True)

        with g.Fori(0, L) as l:
            g.wait_ge(y_v.sem, y_v.at(l, 0))
            g.nop(nofuse=True)
            g.dma_start(PTAB, a["pt"]).then_inc(pt_ld.sem, 16)
            g.dma_start(PRM[:, :], a["prm"][l]).then_inc(prm_ld.sem, 16)
            g.dma_start(AR[:, C_CN:C_CN + NCN], a["cn"]).then_inc(tab_ld.sem, 16)
            g.dma_start(ZALL[:, 47, 0:128], a["wsm"][l]).then_inc(tab_ld.sem, 16)
            g.wait_ge(ho_cp.sem, ho_cp.at(l, 4))
            g.nop(nofuse=True)
            g.dma_start(o["hg_p"][l], W[9]).then_inc(out_st.sem, 16)
            seq_states(l, a["hgs"], o["hg_s"], 0, [wide(0, 1024), wide(2, 1024)])
            g.wait_ge(out_st.sem, out_st.at(l, 16))
            g.nop(nofuse=True)
            g.dma_start(wide(10, 288), a["cvs"][l]).then_inc(cv_ld.sem, 16)
            g.wait_ge(cv_v.sem, cv_v.at(l, 1))
            g.nop(nofuse=True)
            g.dma_start(o["cv"][l], RO[:, 2, 0:324]).then_inc(out_st.sem, 16)
            g.wait_ge(g_v.sem, g_v.at(l, 4 * 18))
            g.nop(nofuse=True)
            g.dma_start(o["gd_p"][l], W[9]).then_inc(out_st.sem, 16)
            seq_states(l, a["gds"], o["gd_s"], 4, [AR[:, C_SQ:C_SQ + 1024], AR[:, C_SQ + 1024:C_SQ + 2048]])
            g.wait_ge(fx_r.sem, fx_r.at(l, 1))
            g.nop(nofuse=True)
            g.dma_start(o["fk"][l], KBs).then_inc(out_st.sem, 16)
            g.dma_start(o["fv"][l], VBs).then_inc(out_st.sem, 16)
            g.dma_start(o["fl"][l], R_L[0:8, :]).then_inc(out_st.sem, 16)
            g.wait_ge(pt_ld.sem, pt_ld.at(l, 16))
            g.nop(nofuse=True)
            for q in range(NSEQ):
                g.dma_start(LG[8 * q:8 * q + 8, PAST:PAST + TS], R_L[0:8, TP + TS * q:TP + TS * (q + 1)]).then_inc(ln_ld.sem, 16)
                for pg in range(NPG):
                    r = g.value_load(PTAB[0:1, q * NPG + pg:q * NPG + pg + 1], min_val=0, max_val=a["ck"].shape[1] - 1)
                    g.dma_start(LG[8 * q:8 * q + 8, pg * PAGE:(pg + 1) * PAGE], a["cl"][l, r]).then_inc(lg_ld.sem, 16)
            g.wait_ge(ft_cp.sem, ft_cp.at(l, 4))
            g.nop(nofuse=True)
            g.wait_ge(out_st.sem, out_st.at(l, 16 * 6))
            g.nop(nofuse=True)
            g.wait_ge(ln_ld.sem, ln_ld.at(l, 16 * 8))
            g.nop(nofuse=True)
            for q in range(NSEQ):
                if q >= 2:
                    g.wait_ge(qo_mm.sem, qo_mm.at(l, q - 1))
                    g.nop(nofuse=True)
                for pg in range(NPG):
                    r = g.value_load(PTAB[0:1, q * NPG + pg:q * NPG + pg + 1], min_val=0, max_val=a["ck"].shape[1] - 1)
                    g.dma_start(v_page(q, pg), a["cvv"][l, r]).then_inc(vc_ld[q % 2].sem, 16)
        g.wait_ge(y_v.sem, y_v.at(L - 1, 16))
        g.nop(nofuse=True)
        g.dma_start(o["x"], xT[:, :, :]).then_inc(out_st.sem, 16)
        g.wait_ge(out_st.sem, L * 16 * 6 + 16)
        g.wait_ge(ss_st.sem, L * ss_st.n)

    @block.tensor
    def _(pe):
        mm = nc.tensor.matmul
        tr = nc.tensor.transpose

        def spread(row):
            return ident[0:16, row:row + 1].to_broadcast([16, P])

        def chunk_mm(dst, w, src):
            for hf in range(2):
                for c in range(DC):
                    i = mm(dst[:, hf, :], w[:, c, :], src[:, c, hf * HT:(hf + 1) * HT], start=(c == 0), stop=(c == DC - 1))
            return i

        def norm_mm(l, n, src):
            pe.wait_ge(sq_r.sem, sq_r.at(l, n + 1))
            pe.nop(nofuse=True)
            for hf in range(2):
                for c in range(DC):
                    i = mm(PS[:, 4 + hf, 0:HT], ones[:, :], src[:, c, hf * HT:(hf + 1) * HT], start=(c == 0), stop=(c == DC - 1))
            i.then_inc(ms_mm.sem, 1)

        def headnorm(l, g):
            base, R = HN_BASE[g], HN_ROWS[g]
            if base:
                pe.wait_ge(hn_ap.sem, hn_ap.at(l, base))
                pe.nop(nofuse=True)
            for n, (_, sel, row, k, _) in enumerate(HN[g]):
                mid = (CN[sel][1] - k) // 2
                pe.wait_ge(hn_sq.sem, hn_sq.at(l, base + n + 1))
                pe.nop(nofuse=True)
                for hf in range(2):
                    i = mm(PS[0:R, 4 + hf, 0:HT], cn(sel)[:, mid - row:mid - row + R], SQ[n % 2][:, hf * HT:(hf + 1) * HT],
                           start=(n == 0), stop=(n == len(HN[g]) - 1))
                i.then_inc(hn_mm.sem, 1)
            pe.wait_ge(hn_rc.sem, hn_rc.at(l, g + 1))
            pe.nop(nofuse=True)
            for n, (_, sel, row, k, _) in enumerate(HN[g]):
                if n >= 2:
                    pe.wait_ge(hn_ap.sem, hn_ap.at(l, base + n - 1))
                    pe.nop(nofuse=True)
                w = ident[0:R, row:row + 1].to_broadcast([R, P]) if k == 1 else wide(10, 1024)[0:R, (n - 4) * P:(n - 3) * P]
                for hf in range(2):
                    i = mm(PS[:, 6 - 2 * (n % 2) + hf, 0:HT], w, SQ[3][0:R, hf * HT:(hf + 1) * HT], start=True, stop=True)
                i.then_inc(hn_sp.sem, 1)

        pe.wait_ge(init_c, 1)
        pe.drain().then_inc(oh_mm.sem, oh_mm.first)
        with pe.Fori(0, L) as l:
            pe.wait_ge(y_v.sem, y_v.at(l, 0))
            pe.nop(nofuse=True)
            with pe.Fori(0, G_ADA) as k:
                for s in range(RING):
                    pe.wait_ge(ring_full[s], tiles_in(l, k))
                    for c in range(DC):
                        i = mm(PS[:, 7, bass.ds((k * 4 + s) * 9, 9)], ring[:, s, c, :], cT[:, c, :], start=(c == 0), stop=(c == DC - 1))
                    i.then_inc(ring_used[s], 1)
            norm_mm(l, 0, XSQ)
            pe.wait_ge(h_r.sem, h_r.at(l, 1))
            pe.nop(nofuse=True)
            pe.wait_ge(tab_ld.sem, tab_ld.at(l, 32))
            pe.nop(nofuse=True)
            wsm = ZALL[:, 47, 0:128].rearrange("p (c r) -> p c r", c=DC)
            for hf in range(2):
                for c in range(DC):
                    i = mm(PS[0:16, 6 + hf, 0:HT], wsm[:, c, :], hT[:, c, hf * HT:(hf + 1) * HT], start=(c == 0), stop=(c == DC - 1))
            i.then_inc(zs_mm.sem, 1)
            with pe.Fori(0, G_Z) as k:
                for s in range(RING):
                    pe.wait_ge(ring_full[s], tiles_in(l, k + B_Z))
                    pe.wait_ge(z_ev.sem, z_ev.at(l, k * 4 + (s - 1)))
                    chunk_mm(pair(2 * (s % 2)), ring[:, s, :, :], hT).then_inc(ring_used[s], 1)
            pe.wait_ge(zs_r.sem, zs_r.at(l, 1))
            pe.nop(nofuse=True)
            n = 0
            for lv in range(8):
                pe.wait_ge(hg_lvl.sem, hg_lvl.at(l, lv + 1))
                pe.nop(nofuse=True)
                for p in range(5 if lv < 3 else 4):
                    c0, w = NTS[p]
                    pe.wait_ge(att_cp.sem, att_cp.at(l, n - 3))
                    pe.nop(nofuse=True)
                    for h in range(H):
                        i = mm(PS[0:w, 4 + n % 4, h * w:(h + 1) * w], Ks[:, h, c0:c0 + w], Qs[:, h, c0:c0 + w], start=True, stop=True)
                    i.then_inc(att_mm.sem, 1)
                    n += 1
            pe.wait_ge(hg_lvl.sem, hg_lvl.at(l, 9))
            pe.nop(nofuse=True)
            pe.wait_ge(z_ev.sem, z_ev.at(l, 44))
            pe.nop(nofuse=True)
            pe.wait_ge(att_cp.sem, att_cp.at(l, 35))
            pe.nop(nofuse=True)
            for p in range(5):
                c0, w = NTS[p]
                vt, kt = W[5 + p % 2], W[7 + p % 2]
                if p >= 2:
                    pe.wait_ge(hv_cp.sem, hv_cp.at(l, p - 1))
                    pe.nop(nofuse=True)
                for h in range(H):
                    tr(PS[0:w, 2 * (p % 2), h * P:(h + 1) * P], Is[:, h, c0:c0 + w], ident[:, :])
                    i = tr(PS[0:w, 2 * (p % 2) + 1, h * P:(h + 1) * P], Ks[:, h, c0:c0 + w], ident[:, :])
                i.then_inc(hv_mm.sem, 1)
                pe.wait_ge(hv_cp.sem, hv_cp.at(l, p + 1))
                pe.nop(nofuse=True)
                if p < NT:
                    if p:
                        pe.wait_ge(ho_cp.sem, ho_cp.at(l, p))
                        pe.nop(nofuse=True)
                    for h in range(H):
                        hs = slice(h * P, (h + 1) * P)
                        if p:
                            mm(PS[:, 4 + p % 2, hs], W[9][:, hs], Qs[:, h, c0:c0 + w], start=True, stop=False)
                        mm(PS[:, 4 + p % 2, hs], vt[:, hs], W[p][:, hs], start=(p == 0), stop=True)
                        i = mm(PS[:, 6 + p % 2, hs], kt[:, hs], vt[:, hs], start=True, stop=True)
                    i.then_inc(ho_mm.sem, 1)
                else:
                    pe.wait_ge(ho_cp.sem, ho_cp.at(l, 4))
                    pe.nop(nofuse=True)
                    for h in range(H):
                        hs, ho = slice(h * P, (h + 1) * P), slice(h * TSA, (h + 1) * TSA)
                        st = wide(2 * (h % 2), 1024)
                        pe.wait_ge(ss_ld[h % 2].sem, ss_ld[h % 2].at(l, 16 * (h // 2 + 1)))
                        pe.nop(nofuse=True)
                        pe.wait_ge(bd_r.sem, bd_r.at(l, h + 1))
                        pe.nop(nofuse=True)
                        mm(PS[:, 4, ho], vt[0:32, hs], W[4][0:32, ho], start=True, stop=True)
                        for q in range(NSEQ):
                            i = mm(PS[:, 4, h * TSA + q * TS:h * TSA + (q + 1) * TS], st[:, q * P:(q + 1) * P],
                                   Qs[:, h, TP + q * TS:TP + (q + 1) * TS], start=False, stop=True, skip_group_check=True)
                        if h == H - 1:
                            i.then_inc(so_mm.sem, 1)
                        if h:
                            pe.wait_ge(ss_up.sem, ss_up.at(l, h))
                            pe.nop(nofuse=True)
                        mm(PS[:, 6, :], kt[0:32, hs], wide(10, 1024)[0:32, 0:512], start=True, stop=True)
                        mm(PS[:, 7, :], kt[0:32, hs], wide(10, 1024)[0:32, 512:1024], start=True, stop=True).then_inc(sd_mm.sem, 1)
            pe.wait_ge(ss_up.sem, ss_up.at(l, 4))
            pe.nop(nofuse=True)
            headnorm(l, 0)
            headnorm(l, 1)
            pe.wait_ge(hn_ap.sem, hn_ap.at(l, 12))
            pe.nop(nofuse=True)
            pe.wait_ge(rw_x.sem, rw_x.at(l, 1))
            pe.nop(nofuse=True)
            for p in range(5):
                c0, w = NTS[p]
                for j, r in enumerate((R_G, R_B, R_E, R_D)):
                    i = tr(PS[0:w, 0, p * 64 + j * 16:p * 64 + (j + 1) * 16], r[:, c0:c0 + w], ident[0:16, 0:16])
            i.then_inc(ct_mm.sem, 1)
            for j in range(8):
                h, row, src = (j % 4, 12, R_B) if j < 4 else (j % 4, 8, R_E)
                if j >= 2:
                    pe.wait_ge(bc_v.sem, bc_v.at(l, j - 1))
                    pe.nop(nofuse=True)
                for hf in range(2):
                    i = mm(PS[:, 4 + 2 * (j % 2) + hf, 0:HT], spread(row + h), src[:, hf * HT:(hf + 1) * HT], start=True, stop=True)
                i.then_inc(bc_mm.sem, 1)
            pe.wait_ge(gq_r.sem, gq_r.at(l, 1))
            pe.nop(nofuse=True)
            pe.wait_ge(ct_r.sem, ct_r.at(l, 1))
            pe.nop(nofuse=True)
            for p in range(5):
                c0, w = NTS[p]
                V0, S0, cs = p * 18, p * 8, slice(c0, c0 + w)

                def four(bank, lhs, rhs):
                    for h in range(H):
                        ho = slice(h * w, (h + 1) * w)
                        i = mm(PS[0:w, bank, ho], lhs[0:w, ho], rhs[0:w, ho], start=True, stop=True)
                    return i

                for h in range(H):
                    i = mm(PS[:, 0, h * w:(h + 1) * w], spread(8 + h), R_G[:, cs], start=True, stop=True)
                i.then_inc(g_mm.sem, 1)
                for h in range(H):
                    mm(PS[0:w, 1, h * w:(h + 1) * w], KCs[:, h, cs], KBETA[:, h, cs], start=True, stop=True)
                for h in range(H):
                    i = mm(PS[0:w, 2, h * w:(h + 1) * w], KCs[:, h, cs], QCs[:, h, cs], start=True, stop=True)
                i.then_inc(g_mm.sem, 1)
                pe.wait_ge(g_v.sem, g_v.at(l, V0 + 2))
                pe.nop(nofuse=True)
                for h in range(H):
                    i = tr(PS[0:w, 3, h * w:(h + 1) * w], W[4][0:w, h * w:(h + 1) * w], ident[0:w, 0:w])
                i.then_inc(g_mm.sem, 1)
                pe.wait_ge(g_s.sem, g_s.at(l, S0 + 2))
                pe.nop(nofuse=True)
                four(4, W[4], W[5])
                four(5, W[5], W[4]).then_inc(g_mm.sem, 1)
                pe.wait_ge(g_s.sem, g_s.at(l, S0 + 3))
                pe.nop(nofuse=True)
                pe.wait_ge(g_v.sem, g_v.at(l, V0 + 4))
                pe.nop(nofuse=True)
                four(6, W[6], W[7])
                four(7, W[7], W[6])
                four(0, W[7], W[8]).then_inc(g_mm.sem, 1)
                pe.wait_ge(g_s.sem, g_s.at(l, S0 + 4))
                pe.nop(nofuse=True)
                pe.wait_ge(g_v.sem, g_v.at(l, V0 + 6))
                pe.nop(nofuse=True)
                four(1, W[4], W[5])
                four(2, W[5], W[8]).then_inc(g_mm.sem, 1)
                pe.wait_ge(g_s.sem, g_s.at(l, S0 + 5))
                pe.nop(nofuse=True)
                pe.wait_ge(g_v.sem, g_v.at(l, V0 + 7))
                pe.nop(nofuse=True)
                four(3, W[6], W[8]).then_inc(g_mm.sem, 1)
                pe.wait_ge(g_v.sem, g_v.at(l, V0 + 8))
                pe.nop(nofuse=True)
                for h in range(H):
                    i = tr(PS[0:w, 4, h * w:(h + 1) * w], W[8][0:w, h * w:(h + 1) * w], ident[0:w, 0:w])
                i.then_inc(g_mm.sem, 1)
                for lv in range(3):
                    pe.wait_ge(g_v.sem, g_v.at(l, V0 + 9 + 3 * lv))
                    pe.nop(nofuse=True)
                    if lv == 0:
                        pe.wait_ge(g_s.sem, g_s.at(l, S0 + 6))
                        pe.nop(nofuse=True)
                    four(5, W[4], W[10]).then_inc(g_mm.sem, 1)
                    pe.wait_ge(g_v.sem, g_v.at(l, V0 + 10 + 3 * lv))
                    pe.nop(nofuse=True)
                    four(6, W[5], W[8])
                    four(7, W[8], W[5]).then_inc(g_mm.sem, 1)
                pe.wait_ge(g_v.sem, g_v.at(l, V0 + 17))
                pe.nop(nofuse=True)
                for h in range(H):
                    tr(PS[0:w, 0, h * P:(h + 1) * P], KCs[:, h, cs], ident[:, :])
                    i = tr(PS[0:w, 1, h * P:(h + 1) * P], VCs[:, h, cs], ident[:, :])
                i.then_inc(g_mm.sem, 1)
                pe.wait_ge(gk_r.sem, gk_r.at(l, p + 1))
                pe.nop(nofuse=True)
                for h in range(H):
                    i = mm(PS[:, 2, h * w:(h + 1) * w], W[4][0:w, h * P:(h + 1) * P], W[8][0:w, h * w:(h + 1) * w], start=True, stop=True)
                i.then_inc(g_mm.sem, 1)
                pe.wait_ge(g_s.sem, g_s.at(l, S0 + 7))
                pe.nop(nofuse=True)
                if p:
                    pe.wait_ge(g_v.sem, g_v.at(l, V0))
                    pe.nop(nofuse=True)
                if p < NT:
                    for h in range(H):
                        hs = slice(h * P, (h + 1) * P)
                        i = mm(PS[:, 3, hs], W[8][:, hs], W[7][:, hs], start=True, stop=(p == 0))
                        if p:
                            i = mm(PS[:, 3, hs], W[1][:, hs], W[9][:, hs], start=False, stop=True)
                    i.then_inc(g_mm.sem, 1)
                    pe.wait_ge(g_s.sem, g_s.at(l, S0 + 8))
                    pe.nop(nofuse=True)
                    for h in range(H):
                        hs = slice(h * P, (h + 1) * P)
                        if p:
                            mm(PS[:, 4, hs], W[9][:, hs], QE[:, h, cs], start=True, stop=False)
                        mm(PS[:, 4, hs], W[11][:, hs], W[2][:, hs], start=(p == 0), stop=True)
                        i = mm(PS[:, 5, hs], W[12][:, hs], W[11][:, hs], start=True, stop=True)
                    i.then_inc(g_mm.sem, 1)
                else:
                    for h in range(H):
                        hs, ho = slice(h * P, (h + 1) * P), slice(h * TSA, (h + 1) * TSA)
                        st = AR[:, C_SQ + 1024 * (h % 2):C_SQ + 1024 * (h % 2 + 1)]
                        wm = W[0 if h < 2 else 3][:, (h % 2) * 256:(h % 2 + 1) * 256]
                        pe.wait_ge(ss_ld[h % 2].sem, ss_ld[h % 2].at(l, 16 * (2 + h // 2 + 1)))
                        pe.nop(nofuse=True)
                        pe.wait_ge(gw_r.sem, gw_r.at(l, h + 1))
                        pe.nop(nofuse=True)
                        mm(PS[0:32, 3, hs], W[8][0:32, ho], W[7][0:32, hs], start=True, stop=False)
                        for q in range(NSEQ):
                            i = mm(PS[0:32, 3, hs], wm[:, q * 32:(q + 1) * 32], st[:, q * P:(q + 1) * P], start=False, stop=(q == NSEQ - 1))
                        i.then_inc(gu_mm.sem, 1)
                        pe.wait_ge(bd_r.sem, bd_r.at(l, 4 + h + 1))
                        pe.nop(nofuse=True)
                        mm(PS[:, 4, ho], W[11][0:32, hs], W[2][0:32, ho], start=True, stop=True)
                        for q in range(NSEQ):
                            i = mm(PS[:, 4, h * TSA + q * TS:h * TSA + (q + 1) * TS], st[:, q * P:(q + 1) * P],
                                   QE[:, h, TP + q * TS:TP + (q + 1) * TS], start=False, stop=True, skip_group_check=True)
                        if h == H - 1:
                            i.then_inc(so_mm.sem, 1)
                        pe.wait_ge(ss_up.sem, ss_up.at(l, 4 + h))
                        pe.nop(nofuse=True)
                        mm(PS[:, 6, :], W[12][0:32, hs], wide(5, 1024)[0:32, 0:512], start=True, stop=True)
                        mm(PS[:, 7, :], W[12][0:32, hs], wide(5, 1024)[0:32, 512:1024], start=True, stop=True).then_inc(sd_mm.sem, 1)
            pe.wait_ge(ss_up.sem, ss_up.at(l, 8))
            pe.nop(nofuse=True)
            headnorm(l, 2)
            pe.wait_ge(oc_r.sem, oc_r.at(l, 1))
            pe.nop(nofuse=True)
            pe.wait_ge(fx_r.sem, fx_r.at(l, 1))
            pe.nop(nofuse=True)
            for p in range(5):
                c0, w = NTS[p]
                if p >= 2:
                    pe.wait_ge(fv_cp.sem, fv_cp.at(l, p - 1))
                    pe.nop(nofuse=True)
                for c in range(4):
                    i = tr(PS[0:w, p % 2, c * P:(c + 1) * P], VBs[:, c, c0:c0 + w], ident[:, :])
                i.then_inc(fv_mm.sem, 1)
            pe.wait_ge(fv_cp.sem, fv_cp.at(l, 5))
            pe.nop(nofuse=True)

            def fox_scores(j):
                i, h = j // HB, j % HB
                hp, N = slice(64 * (h % 2), 64 * (h % 2) + 64), (i + 1) * P
                if j >= 2:
                    pe.wait_ge(fs_ex.sem, fs_ex.at(l, j - 1))
                    pe.nop(nofuse=True)
                b = j % 2
                mm(PS[:, b, 0:N], QBs[hp, h // 2, i * P:(i + 1) * P], KBs[hp, h // 2, 0:N], start=True, stop=False)
                mm(PS[:, b, i * P:N], ident[:, :], cn("neg"), start=False, stop=False, skip_group_check=True)
                mm(PS[:, b, 0:N], cn("nsel")[0:16, h:h + 1].to_broadcast([16, P]), R_F[:, 0:N], start=False, stop=True).then_inc(fs_mm.sem, 1)

            for j in range(4 * HB):
                i, h = j // HB, j % HB
                if j == 0:
                    fox_scores(0)
                pe.wait_ge(fs_ex.sem, fs_ex.at(l, j + 1))
                pe.nop(nofuse=True)
                if j >= 2:
                    pe.wait_ge(fp_cp.sem, fp_cp.at(l, j - 1))
                    pe.nop(nofuse=True)
                for k in range(i + 1):
                    t_ = tr(PS[:, 2 + j % 2, k * P:(k + 1) * P], W[5 + j % 2][:, k * P:(k + 1) * P], ident[:, :])
                t_.then_inc(fp_mm.sem, 1)
                if j + 1 < 4 * HB and (j + 1) % HB:
                    fox_scores(j + 1)
                pe.wait_ge(fp_cp.sem, fp_cp.at(l, j + 1))
                pe.nop(nofuse=True)
                if h == 0 and i >= 2:
                    pe.wait_ge(fn_r.sem, fn_r.at(l, i - 1))
                    pe.nop(nofuse=True)
                for k in range(i + 1):
                    t_ = mm(PS[:, 4 + i % 2, h * 64:(h + 1) * 64], W[7 + j % 2][:, k * P:(k + 1) * P], W[k][:, h * 64:(h + 1) * 64],
                            start=(k == 0), stop=(k == i))
                t_.then_inc(fo_mm.sem, 1)
                if h == HB - 1:
                    pe.wait_ge(fn_r.sem, fn_r.at(l, i + 1))
                    pe.nop(nofuse=True)
                    if i:
                        pe.wait_ge(ft_cp.sem, ft_cp.at(l, i))
                        pe.nop(nofuse=True)
                    for c in range(4):
                        t_ = tr(PS[:, 6, c * P:(c + 1) * P], W[10][:, c * P:(c + 1) * P], ident[:, :])
                    t_.then_inc(ft_mm.sem, 1)
                    if j + 1 < 4 * HB:
                        fox_scores(j + 1)
            pe.wait_ge(ft_cp.sem, ft_cp.at(l, 4))
            pe.nop(nofuse=True)
            pe.wait_ge(lg_r.sem, lg_r.at(l, 1))
            pe.nop(nofuse=True)
            QBD = wide(2, 1024).rearrange("p (q c m) -> p q c m", q=NSEQ, c=4)
            sel8 = cn("sel8").rearrange("p (q m) -> p q m", q=NSEQ)
            ms = cn("ms").rearrange("p (q m) -> p q m", q=NSEQ)

            def seq_scores(q):
                pe.wait_ge(kc_ld[q % 2].sem, kc_ld[q % 2].at(l, 16 * 8 * (q // 2 + 1)))
                pe.nop(nofuse=True)
                for b in range(3):
                    N, ks = (512, slice(b * 512, (b + 1) * 512)) if b < 2 else (TSA, slice(0, 0))
                    for c in range(4):
                        rhs = k_pages(q)[:, c, ks] if b < 2 else KBs[:, c, TP:T]
                        mm(PS[0:32, b, 0:N], QBD[:, q, c, :], rhs, start=(c == 0), stop=False)
                    rhs = LG[0:64, ks] if b < 2 else LG[0:64, PAST:PAST + TS].unsqueeze(1).to_broadcast([64, NSEQ, TS])
                    i = mm(PS[0:32, b, 0:N], sel8[0:64, q, :], rhs, start=False, stop=(b < 2))
                    if b == 2:
                        i = mm(PS[0:32, b, 0:N], ident[0:32, 0:32], ms[0:32, q, :], start=False, stop=True)
                i.then_inc(qs_mm.sem, 1)

            def seq_out(q):
                pe.wait_ge(qn_r.sem, qn_r.at(l, q + 1))
                pe.nop(nofuse=True)
                if q:
                    pe.wait_ge(qt_cp.sem, qt_cp.at(l, q))
                    pe.nop(nofuse=True)
                for c in range(4):
                    i = mm(PS[:, 5, c * TS:(c + 1) * TS], W[0][0:32, c * P:(c + 1) * P], cn("selt")[0:32, :], start=True, stop=True)
                i.then_inc(qt_mm.sem, 1)

            seq_scores(0)
            for q in range(NSEQ):
                pe.wait_ge(qs_ex.sem, qs_ex.at(l, q + 1))
                pe.nop(nofuse=True)
                for k in range(8):
                    tr(PS[:, 3, k * 32:(k + 1) * 32], probs1(q)[0:32, k * P:(k + 1) * P], ident[0:32, 0:32])
                tr(PS[0:32, 3, 256:288], probs1(q)[0:32, PAST:PAST + 32], ident[0:32, 0:32]).then_inc(qp_mm.sem, 1)
                if q + 1 < NSEQ:
                    seq_scores(q + 1)
                if q:
                    seq_out(q - 1)
                pe.wait_ge(qp_cp.sem, qp_cp.at(l, q + 1))
                pe.nop(nofuse=True)
                pe.wait_ge(vc_ld[q % 2].sem, vc_ld[q % 2].at(l, 16 * 8 * (q // 2 + 1)))
                pe.nop(nofuse=True)
                for k in range(8):
                    mm(PS[0:32, 4, :], W[1][:, k * 32:(k + 1) * 32], v_page(q, k), start=(k == 0), stop=False)
                mm(PS[0:32, 4, :], W[1][0:32, 256:288], W[4][0:32, :], start=False, stop=True).then_inc(qo_mm.sem, 1)
            seq_out(NSEQ - 1)
            pe.wait_ge(oa_r.sem, oa_r.at(l, 1))
            pe.nop(nofuse=True)
            pe.wait_ge(qt_cp.sem, qt_cp.at(l, 8))
            pe.nop(nofuse=True)
            with pe.Fori(0, 2) as kc:
                for c4 in range(4):
                    for st in range(3):
                        m = 3 * c4 + st
                        gs = 5 * c4 + (0, 2, 3)[st]
                        ys = 5 * c4 + (1, 1, 4)[st]
                        pe.wait_ge(mg_v.sem, mg_v.at(l, kc * 12 + (m - 1)))
                        pe.wait_ge(ring_full[gs % 4], tiles_in(l, kc * 5 + (B_MG + gs // 4)))
                        chunk_mm(pair(4 * (m % 2)), ring[:, gs % 4, :, :], hT).then_inc(ring_used[gs % 4], 1)
                        if st != 1:
                            pe.wait_ge(ring_full[ys % 4], tiles_in(l, kc * 5 + (B_MG + ys // 4)))
                        src = (Qs, QBs, VCs)[st]
                        for hf in range(2):
                            for c in range(4):
                                i = mm(PS[:, 4 * (m % 2) + 2 + hf, 0:HT], ring[:, ys % 4, (4 if st == 1 else 0) + c, :],
                                       src[:, c, hf * HT:(hf + 1) * HT], start=(c == 0), stop=(c == 3))
                        if st == 0:
                            i.then_inc(mg_mm.sem, 1)
                        else:
                            i.then_inc(ring_used[ys % 4], 1)
            pe.wait_ge(mg_v.sem, mg_v.at(l, 24))
            pe.nop(nofuse=True)
            with pe.Fori(0, 2) as k:
                for s in range(RING):
                    pe.wait_ge(ring_full[s], tiles_in(l, k + B_OUT))
                    pe.wait_ge(wo_v.sem, wo_v.at(l, k * 4 + (s - 1)))
                    chunk_mm(pair(2 * (s % 2)), ring[:, s, :, :], MG).then_inc(ring_used[s], 1)
            norm_mm(l, 1, XSQ)
            pe.wait_ge(h_r.sem, h_r.at(l, 2))
            pe.nop(nofuse=True)
            with pe.Fori(0, 4) as k:
                for s in range(RING):
                    pe.wait_ge(ring_full[s], tiles_in(l, k + B_Q))
                    pe.wait_ge(qj_s.sem, qj_s.at(l, k * 4 + (s - 1)))
                    chunk_mm(pair(2 * (s % 2)), ring[:, s, :, :], hT).then_inc(ring_used[s], 1)
            pe.wait_ge(qj_s.sem, qj_s.at(l, 16))
            pe.nop(nofuse=True)
            keys = pr("keys").rearrange("p (a n) -> p a n", a=2)

            def routes_t(p):
                c0, w = NTS[p]
                pe.wait_ge(rt_v.sem, rt_v.at(l, p + 1))
                pe.nop(nofuse=True)
                for j in range(3):
                    i = tr(PS[:, 4, j * P:j * P + w], W[j][0:w, 0:P], ident[0:w, 0:w])
                i.then_inc(rr_mm.sem, 1)

            for p in range(5):
                c0, w = NTS[p]
                if p:
                    pe.wait_ge(sc_s.sem, sc_s.at(l, p))
                    pe.nop(nofuse=True)
                for j in range(16):
                    i = mm(PS[0:w, j // 4, (j % 4) * P:(j % 4 + 1) * P], QP[:, j, c0:c0 + w], keys[:, j % 2, :], start=True, stop=True)
                i.then_inc(sc_mm.sem, 1)
                if p:
                    if p > 1:
                        pe.wait_ge(rr_s.sem, rr_s.at(l, p - 1))
                        pe.nop(nofuse=True)
                    routes_t(p - 1)
            pe.wait_ge(rr_s.sem, rr_s.at(l, 4))
            pe.nop(nofuse=True)
            routes_t(4)
            for hf in range(2):
                with pe.Fori(0, 34) as k:
                    for b in range(2):
                        pe.wait_ge(oi_v.sem, oi_v.at(l, k * 2 + (hf * 68 + b + 1)))
                        pe.wait_ge(oj_s.sem, oj_s.at(l, k * 2 + (hf * 68 + b + 1)))
                        pe.wait_ge(w_ev.sem, w_ev.at(l, k * 2 + (hf * 68 + b - 1)))
                        for j in range(4):
                            i = mm(PS[:, b, j * P:(j + 1) * P], OHJ[b][:, j, :], OHI[b][:, j, :], start=True, stop=True)
                        i.then_inc(oh_mm.sem, 1)
                with pe.Fori(0, G_U) as k:
                    for s in range(RING):
                        pe.wait_ge(ring_full[s], tiles_in(l, k + (G_W + hf * (G_U + G_V))))
                        pe.wait_ge(gl_s.sem, gl_s.at(l, k * 4 + (hf * 128 + s - 1)))
                        for c in range(DC):
                            i = mm(PS[:, 2 + s % 2, 0:HT], ring[:, s, c, :], hT[:, c, hf * HT:(hf + 1) * HT], start=(c == 0), stop=(c == DC - 1))
                        i.then_inc(ring_used[s], 1)
                pe.wait_ge(a_v.sem, a_v.at(l, (hf + 1) * 128))
                pe.nop(nofuse=True)
                with pe.Fori(0, 4) as d:
                    for b in range(2):
                        pe.wait_ge(y_v.sem, y_v.at(l, d * 2 + (hf * 8 + b - 1)))

                        def eight(s, k, first, last):
                            pe.wait_ge(ring_full[s], tiles_in(l, (d * 2 + b) * 4 + k + (G_W + hf * (G_U + G_V) + G_U)))
                            for j in range(8):
                                row = (k * 4 + s) * 8 + j
                                i = mm(PS[:, 6 + b, 0:HT], ring[:, s, j, :], WB[:, row, :], start=(first and j == 0), stop=(last and j == 7))
                            i.then_inc(ring_used[s], 1)

                        for k in range(4):
                            for s in range(RING):
                                eight(s, k, k == 0 and s == 0, k == 3 and s == RING - 1)


    NV = nc.vector

    @block.vector
    def _(v):
        tt, ts, stt, cp = NV.tensor_tensor, NV.tensor_scalar, NV.scalar_tensor_tensor, NV.tensor_copy
        bc = lambda ap, shape: ap.to_broadcast(shape)

        NV.memset(epsc[:, 0:1], EPS)
        NV.memset(epsc[:, 2:3], 1.0)
        v.wait_ge(init_ld, 16 * 6)
        cp(wide(0, 4), LB[:, 0, :])
        for i in range(1, L):
            v.drain()
            tt(wide(0, 4), wide(0, 4), LB[:, i, :], ALU.max)
        v.drain()
        tt(LB[:, :, :], LB[:, :, :], bc(wide(0, 4).unsqueeze(1), [P, L, 4]), ALU.subtract)
        v.drain().then_inc(init_v, 1)
        v.wait_ge(init_c, 1)
        cp(wide(0, 4), LB[:, 0, :])
        for i in range(1, L):
            v.drain()
            tt(wide(0, 4), wide(0, 4), LB[:, i, :], ALU.add)
        v.drain()
        NV.reciprocal(wide(0, 4), wide(0, 4))
        v.drain()
        tt(LB[:, :, :], LB[:, :, :], bc(wide(0, 4).unsqueeze(1), [P, L, 4]), ALU.mult)
        v.drain()
        cp(wide(0, 4), LB[:, 0, :])
        for i in range(1, L):
            v.drain()
            tt(LB[:, i, :], LB[:, i, :], LB[:, i - 1, :], ALU.add)
        v.drain()
        tt(LB[:, :, :], LB[:, :, :], bc(wide(0, 4).unsqueeze(1), [P, L, 4]), ALU.subtract)
        v.drain()
        ts(LB[:, :, :], LB[:, :, :], 0.0, None, ALU.max)
        for g_ in (att_cp, mg_v, wo_v, y_v, a_v):
            v.drain().then_inc(g_.sem, g_.first)

        def norm(l, n, sh, sc):
            v.wait_ge(rt_r.sem, rt_r.at(l, n + 1))
            v.nop(nofuse=True)
            rt = SQ[0]
            NV.reciprocal(rt, rt)
            v.drain()
            tt(hT[:, :, :], xT[:, :, :], bc(rt.unsqueeze(1), [P, DC, T]), ALU.mult)
            v.drain()
            for c in range(DC):
                ts(hT[:, c, 0:TP], hT[:, c, 0:TP], MOD[:, sc + c, 0:1], MOD[:, sh + c, 0:1], ALU.mult, ALU.add)
            hs = hT[:, :, TP:T].rearrange("p c (q t) -> p c q t", t=TS)
            tt(hs, hs, bc(MOD[:, sc:sc + DC, 1:9].unsqueeze(3), [P, DC, NSEQ, TS]), ALU.mult)
            v.drain()
            tt(hs, hs, bc(MOD[:, sh:sh + DC, 1:9].unsqueeze(3), [P, DC, NSEQ, TS]), ALU.add)
            v.drain().then_inc(h_r.sem, 1)

        def headnorm(l, g):
            v.wait_ge(hn_rt.sem, hn_rt.at(l, g + 1))
            v.nop(nofuse=True)
            NV.reciprocal(SQ[3][0:HN_ROWS[g], :], SQ[3][0:HN_ROWS[g], :])
            v.drain().then_inc(hn_rc.sem, 1)
            for n, (slot, _, _, _, gain) in enumerate(HN[g]):
                v.wait_ge(hn_sp.sem, hn_sp.at(l, HN_BASE[g] + n + 1))
                v.nop(nofuse=True)
                z, ps = halves(ZALL[:, slot, :]), pair(6 - 2 * (n % 2))
                i = tt(z, z, ps, ALU.mult) if gain is None else stt(z, z, pr(gain), ps, ALU.mult, ALU.mult)
                i.then_inc(hn_ap.sem, 1)
            v.drain()

        def residual(c, g, cols, ps_ap):
            c0, n = cols
            npr = min(c0 + n, TP) - c0
            stt(xT[:, c, c0:c0 + npr], ps_ap[:, 0:npr], MOD[:, g, 0:1], xT[:, c, c0:c0 + npr], ALU.mult, ALU.add)
            if npr < n:
                tmp = rtmp[:, :].rearrange("p (q t) -> p q t", t=TS)
                tt(tmp, ps_ap[:, npr:n].rearrange("p (q t) -> p q t", t=TS), bc(MOD[:, g, 1:9].unsqueeze(2), [P, NSEQ, TS]), ALU.mult)
                v.drain()
                tt(xT[:, c, TP:T], xT[:, c, TP:T], rtmp[:, :], ALU.add)

        with v.Fori(0, L) as l:
            v.wait_ge(prm_ld.sem, prm_ld.at(l, 16))
            v.nop(nofuse=True)
            v.wait_ge(ring_used[RING - 1], tiles_used(l, G_ADA - 1))
            v.nop(nofuse=True)
            tt(MOD[:, :, :], PS[:, 7, 0:432].rearrange("p (a b) -> p a b", b=9), bc(pr("b_ada").unsqueeze(2), [P, 48, 9]), ALU.add)
            v.drain()
            for sc, nm in ((8, "nmix"), (32, "nffn")):
                ts(MOD[:, sc:sc + 8, :], MOD[:, sc:sc + 8, :], 1.0, None, ALU.add)
                v.drain()
                tt(MOD[:, sc:sc + 8, :], MOD[:, sc:sc + 8, :], bc(pr(nm).unsqueeze(2), [P, 8, 9]), ALU.mult)
            v.drain()
            norm(l, 0, 0, 8)
            cp(LBC[:, 0, :], LB[:, l, :])
            v.drain()
            ts(LBC[:, 1, :], LBC[:, 0, :], -1.0, 1.0, ALU.mult, ALU.add)
            v.drain()
            v.wait_ge(z_ev.sem, z_ev.at(l, 12))
            v.nop(nofuse=True)
            for h in range(H):
                ts(Fs[:, h, :], Fs[:, h, :], LBC[:, 1, h:h + 1], LBC[:, 0, h:h + 1], ALU.mult, ALU.add)
                ts(Ks[:, h, :], Ks[:, h, :], LBC[:, 1, h:h + 1], None, ALU.mult)
            v.drain().then_inc(hg_lvl.sem, 1)
            n = 0
            for lv in range(8):
                for p in range(5 if lv < 3 else 4):
                    c0, w = NTS[p]
                    v.wait_ge(att_mm.sem, att_mm.at(l, n + 1))
                    v.nop(nofuse=True)
                    att = W[p][0:w, 0:4 * w].rearrange("p (h t) -> p h t", h=H)
                    src = PS[0:w, 4 + n % 4, 0:4 * w].rearrange("p (h t) -> p h t", h=H)
                    if lv == 0:
                        i = tt(att, src, bc(ident[0:w, 0:w].unsqueeze(1), [w, H, w]), ALU.mult)
                    else:
                        m = cn("lm")[0:w, (lv - 1) * P:(lv - 1) * P + w].bitcast(U32)
                        i = NV.copy_predicated(att, bc(m.unsqueeze(1), [w, H, w]), src)
                    i.then_inc(att_cp.sem, 1)
                    n += 1
                v.drain()
                if lv == 0:
                    tt(Qs, Qs, Fs, ALU.mult)
                else:
                    b = 1 << (lv - 1)
                    wd = T if b <= 2 else TP
                    pairs = lambda z: z[:, :, 0:wd].rearrange("p h (n two b) -> p h n two b", two=2, b=b)
                    D0, D1 = pairs(Fs)[:, :, :, 0, 0:1], pairs(Fs)[:, :, :, 1, 0:1]
                    q1, k0 = pairs(Qs)[:, :, :, 1, :], pairs(Ks)[:, :, :, 0, :]
                    sh = [P, H, wd // (2 * b), b]
                    tt(q1, q1, bc(D0, sh), ALU.mult)
                    tt(k0, k0, bc(D1, sh), ALU.mult)
                    v.drain()
                    tt(D0, D0, D1, ALU.mult)
                v.drain().then_inc(hg_lvl.sem, 1)
            for p in range(NT):
                c0 = p * P
                v.wait_ge(ho_mm.sem, ho_mm.at(l, p + 1))
                v.nop(nofuse=True)
                cp(Qs[:, :, c0:c0 + P], PS[:, 4 + p % 2, :].rearrange("p (h t) -> p h t", h=H))
                for h in range(H):
                    hs = slice(h * P, (h + 1) * P)
                    if p:
                        stt(W[9][:, hs], W[9][:, hs], Fs[:, h, c0:c0 + 1], PS[:, 6 + p % 2, hs], ALU.mult, ALU.add)
                    else:
                        cp(W[9][:, hs], PS[:, 6 + p % 2, hs])
                v.drain().then_inc(ho_cp.sem, 1)

            def seq_update(h, base, st, decay):
                v.wait_ge(sd_mm.sem, sd_mm.at(l, base + h + 1))
                v.nop(nofuse=True)
                st3 = st.rearrange("p (q n) -> p q n", q=NSEQ)
                tt(st3, st3, bc(decay.unsqueeze(2), [P, NSEQ, P]), ALU.mult)
                v.drain()
                tt(st, st, PS[:, 6:8, :].rearrange("p a b -> p (a b)"), ALU.add)
                v.drain().then_inc(ss_up.sem, 1)

            def seq_blocks(dst, src):
                tt(dst[0:32, :].rearrange("p (q n) -> p q n", q=NSEQ), bc(src.unsqueeze(1), [32, NSEQ, P]),
                   bc(cn("sm")[0:32, :].unsqueeze(2), [32, NSEQ, P]), ALU.mult).then_inc(bd_r.sem, 1)

            v.wait_ge(hv_cp.sem, hv_cp.at(l, 5))
            v.nop(nofuse=True)
            for h in range(H):
                seq_blocks(wide(10, 1024), W[5][0:32, h * P:(h + 1) * P])
                seq_update(h, 0, wide(2 * (h % 2), 1024), Fs[:, h, TP:T:TS])
            v.wait_ge(so_mm.sem, so_mm.at(l, 1))
            v.nop(nofuse=True)
            cp(Qs[:, :, TP:T], PS[:, 4, 0:P].rearrange("p (h t) -> p h t", h=H))
            v.drain().then_inc(hn_go.sem, 1)
            headnorm(l, 0)
            tt(Qs, Qs, GAs, ALU.mult)
            v.drain().then_inc(oa_r.sem, 1)
            v.wait_ge(cv_ld.sem, cv_ld.at(l, 16))
            v.nop(nofuse=True)
            v.wait_ge(z_ev.sem, z_ev.at(l, 44))
            v.nop(nofuse=True)
            cw = pr("conv").rearrange("p (j n) -> p j n", j=4)
            raw = slots(S_QC, 12)
            raws = raw[:, :, TP:T].rearrange("p n (q t) -> p n q t", t=TS)
            xp = wide(0, 672).rearrange("p (n q t) -> p n q t", q=NSEQ, t=7)
            acc = wide(2, 384).rearrange("p (n q t) -> p n q t", q=NSEQ, t=TS)
            tmp = wide(3, 384).rearrange("p (n q t) -> p n q t", q=NSEQ, t=TS)
            cp(xp[:, :, :, 0:3], wide(10, 288).rearrange("p (n q t) -> p n q t", q=NSEQ, t=3))
            cp(xp[:, :, :, 3:7], raws)
            cp(CO[:, :, 0:3], raw[:, :, TP - 3:TP])
            cp(CO[:, :, 3:27].rearrange("p n (q t) -> p n q t", t=3), raws[:, :, :, 1:4])
            v.drain()
            for j in range(4):
                tt(acc if j == 0 else tmp, xp[:, :, :, j:j + 4], bc(cw[:, j, :].unsqueeze(2).unsqueeze(3), [P, 12, NSEQ, TS]), ALU.mult)
                v.drain()
                if j:
                    tt(acc, acc, tmp, ALU.add)
                    v.drain()
            v.drain().then_inc(cv_v.sem, 1)
            with v.Fori(0, 6) as k:
                for b in range(2):
                    v.wait_ge(cv_s.sem, cv_s.at(l, k * 2 + b))
                    x = ZALL[:, k * 2 + (S_QC + b), 0:TP]
                    ts(SQ[b][:, 0:TP], x, cw[:, 3, bass.ds(k * 2 + b, 1)], None, ALU.mult)
                    for j in (2, 1, 0):
                        s = 3 - j
                        v.drain()
                        i = stt(SQ[b][:, s:TP], ZALL[:, k * 2 + (S_QC + b), 0:TP - s], cw[:, j, bass.ds(k * 2 + b, 1)], SQ[b][:, s:TP], ALU.mult, ALU.add)
                    i.then_inc(cv_v.sem, 1)
            v.wait_ge(zs_r.sem, zs_r.at(l, 1))
            v.nop(nofuse=True)
            tt(RC[0:16, 0:1], pr("rb")[0:16, :], cn("sgn")[0:16, :], ALU.mult)
            v.drain()
            ts(R_X, ZS, cn("sgn")[0:16, :], RC[0:16, 0:1], ALU.mult, ALU.add)
            v.drain()
            stt(R_Y, R_X, -1.0, R_X, ALU.mult, ALU.min)
            ts(R_L, R_X, 0.0, None, ALU.max)
            v.drain().then_inc(rw_u.sem, 1)
            v.wait_ge(rw_e.sem, rw_e.at(l, 1))
            v.nop(nofuse=True)
            tt(R_L, R_L, R_Y, ALU.add)
            v.drain()
            ts(R_L, R_L, RC[0:16, 1:2], -1.0, ALU.mult, ALU.mult)
            v.drain()
            for p in range(NT):
                NV.tensor_tensor_scan(R_G[:, p * P:(p + 1) * P], bc(ones[0:16, 0:1], [16, P]), R_L[:, p * P:(p + 1) * P], 0.0, ALU.mult, ALU.add)
            NV.tensor_tensor_scan(R_F[:, 0:TP], bc(ones[0:16, 0:1], [16, TP]), R_L[:, 0:TP], 0.0, ALU.mult, ALU.add)
            cp(R_G[:, TP:T], R_L[:, TP:T])
            gs = R_G[:, TP:T].rearrange("p (q t) -> p q t", t=TS)
            for t in range(1, TS):
                v.drain()
                tt(gs[:, :, t:t + 1], gs[:, :, t:t + 1], gs[:, :, t - 1:t], ALU.add)
            v.drain()
            gp = R_G[:, 0:TP].rearrange("p (n t) -> p n t", t=P)
            tt(R_D[:, 0:TP].rearrange("p (n t) -> p n t", t=P), bc(gp[:, :, P - 1:P], [16, NT, P]), gp, ALU.subtract)
            tt(R_D[:, TP:T].rearrange("p (q t) -> p q t", t=TS), bc(gs[:, :, TS - 1:TS], [16, NSEQ, TS]), gs, ALU.subtract)
            v.drain().then_inc(rw_g.sem, 1)
            headnorm(l, 1)
            v.wait_ge(ct_mm.sem, ct_mm.at(l, 1))
            v.nop(nofuse=True)
            cp(CT[:, 0:4, 0:4, :], PS[:, 0, 0:256].rearrange("p (a b c) -> p a b c", b=4, c=16))
            cp(CT[0:32, 4, 0:4, :], PS[0:32, 0, 256:320].rearrange("p (b c) -> p b c", c=16))
            v.drain()
            for n, w in ((slice(0, 4), P), (slice(4, 5), 32)):
                stt(CT[0:w, n, 4, 0:4], CT[0:w, n, 1, 12:16], -1.0, CT[0:w, n, 2, 8:12], ALU.mult, ALU.mult)
            v.drain().then_inc(ct_r.sem, 1)
            for j in range(8):
                h = j % 4
                v.wait_ge(bc_mm.sem, bc_mm.at(l, j + 1))
                v.nop(nofuse=True)
                ps = pair(4 + 2 * (j % 2))
                src, dst = (KCs, KBETA) if j < 4 else (QCs, QE)
                i = tt(halves(dst[:, h, :]), halves(src[:, h, :]), ps, ALU.mult)
                if j >= 4:
                    cp(EGL[:, h, 0:2], ps[:, 0, P - 1:2 * P:P])
                    cp(EGL[:, h, 2:4], ps[:, 1, 3 * P - 1 - HT:4 * P - HT:P])
                    i = cp(EGL[:, h, 4:12], ps[:, 1, TP + TS - 1 - HT:HT:TS])
                i.then_inc(bc_v.sem, 1)
            v.drain().then_inc(gq_r.sem, 1)
            for p in range(5):
                c0, w = NTS[p]
                M0, S0, n4 = p * 18, p * 8, 4 * w
                v3 = lambda ap: ap[0:w, 0:n4].rearrange("p (h t) -> p h t", h=H)
                bk = lambda b: PS[0:w, b, 0:n4]
                m3 = lambda ap: bc(ap[0:w, 0:w].unsqueeze(1), [w, H, w])
                Wn = lambda i: W[i][0:w, 0:n4]
                v.wait_ge(g_mm.sem, g_mm.at(l, M0 + 1))
                v.nop(nofuse=True)
                for h in range(H):
                    ts(W[0][0:w, h * w:(h + 1) * w], PS[0:w, 0, h * w:(h + 1) * w], CT[0:w, p, 0, 8 + h:9 + h], 0.0, ALU.subtract, ALU.min)
                v.drain().then_inc(g_v.sem, 1)
                v.wait_ge(g_mm.sem, g_mm.at(l, M0 + 2))
                v.nop(nofuse=True)
                v.wait_ge(g_s.sem, g_s.at(l, S0 + 1))
                v.nop(nofuse=True)
                tt(v3(W[1]), v3(W[0]), m3(cn("strict") if p < NT else cn("strict4")), ALU.mult)
                tt(v3(W[2]), v3(W[0]), m3(cn("causal") if p < NT else cn("causal4")), ALU.mult)
                v.drain()
                tt(Wn(3), bk(1), Wn(1), ALU.mult)
                tt(Wn(2), bk(2), Wn(2), ALU.mult)
                v.drain()
                tt(v3(W[4]), v3(W[3]), m3(cn("blk16")), ALU.mult)
                v.drain().then_inc(g_v.sem, 1)
                tt(v3(W[8]), m3(ident[:, :]), v3(W[4]), ALU.subtract)
                v.drain().then_inc(g_v.sem, 1)
                v.wait_ge(g_mm.sem, g_mm.at(l, M0 + 4))
                v.nop(nofuse=True)
                cp(Wn(6), bk(5)).then_inc(g_v.sem, 1)
                v.wait_ge(g_mm.sem, g_mm.at(l, M0 + 5))
                v.nop(nofuse=True)
                cp(Wn(4), bk(7)).then_inc(g_v.sem, 1)
                tt(Wn(8), bk(0), Wn(8), ALU.add)
                v.drain().then_inc(g_v.sem, 1)
                v.wait_ge(g_mm.sem, g_mm.at(l, M0 + 6))
                v.nop(nofuse=True)
                tt(Wn(8), bk(2), Wn(8), ALU.add)
                v.drain().then_inc(g_v.sem, 1)
                v.wait_ge(g_mm.sem, g_mm.at(l, M0 + 7))
                v.nop(nofuse=True)
                tt(Wn(8), bk(3), Wn(8), ALU.add)
                v.drain().then_inc(g_v.sem, 1)
                for lv in range(3):
                    lm = cn("lm")[:, (4 + lv) * P:(5 + lv) * P]
                    tt(v3(W[4]), v3(W[3]), m3(lm), ALU.mult).then_inc(g_v.sem, 1)
                    v.wait_ge(g_mm.sem, g_mm.at(l, M0 + 9 + 2 * lv))
                    v.nop(nofuse=True)
                    cp(Wn(5), bk(5)).then_inc(g_v.sem, 1)
                    v.wait_ge(g_mm.sem, g_mm.at(l, M0 + 10 + 2 * lv))
                    v.nop(nofuse=True)
                    tt(Wn(8), Wn(8), bk(6), ALU.subtract)
                    tt(Wn(10), Wn(10), bk(7), ALU.subtract)
                    v.drain().then_inc(g_v.sem, 1)
                v.wait_ge(g_mm.sem, g_mm.at(l, M0 + 15))
                v.nop(nofuse=True)
                for h in range(H):
                    hs = slice(h * P, (h + 1) * P)
                    ts(W[4][0:w, hs], PS[0:w, 0, hs], CT[0:w, p, 4, h:h + 1], None, ALU.mult)
                    ts(W[12][0:w, hs], PS[0:w, 0, hs], CT[0:w, p, 3, 8 + h:9 + h], None, ALU.mult)
                    ts(W[7][0:w, hs], PS[0:w, 1, hs], CT[0:w, p, 1, 12 + h:13 + h], None, ALU.mult)
                v.drain().then_inc(gk_r.sem, 1)
                if p < NT:
                    v.wait_ge(g_mm.sem, g_mm.at(l, M0 + 18))
                    v.nop(nofuse=True)
                    cp(VCs[:, :, c0:c0 + P], PS[:, 4, :].rearrange("p (h t) -> p h t", h=H))
                    for h in range(H):
                        hs = slice(h * P, (h + 1) * P)
                        if p:
                            stt(W[9][:, hs], W[9][:, hs], EGL[:, h, p:p + 1], PS[:, 5, hs], ALU.mult, ALU.add)
                        else:
                            cp(W[9][:, hs], PS[:, 5, hs])
                    v.drain().then_inc(g_v.sem, 1)
                else:
                    v.wait_ge(g_s.sem, g_s.at(l, S0 + 7))
                    v.nop(nofuse=True)
                    for h in range(H):
                        wm = W[0 if h < 2 else 3][:, (h % 2) * 256:(h % 2 + 1) * 256].rearrange("p (q t) -> p q t", q=NSEQ)
                        tt(wm, bc(W[1][:, h * 32:(h + 1) * 32].unsqueeze(1), [P, NSEQ, 32]),
                           cn("smk").rearrange("p (q t) -> p q t", q=NSEQ), ALU.mult).then_inc(gw_r.sem, 1)
                    for h in range(H):
                        v.wait_ge(gu_s.sem, gu_s.at(l, h + 1))
                        v.nop(nofuse=True)
                        seq_blocks(wide(5, 1024), W[11][0:32, h * P:(h + 1) * P])
                        seq_update(h, 4, AR[:, C_SQ + 1024 * (h % 2):C_SQ + 1024 * (h % 2 + 1)], EGL[:, h, 4:12])
            v.wait_ge(so_mm.sem, so_mm.at(l, 2))
            v.nop(nofuse=True)
            cp(VCs[:, :, TP:T], PS[:, 4, 0:P].rearrange("p (h t) -> p h t", h=H))
            cp(wide(10, 1024)[0:20, :].rearrange("p (n d) -> p n d", d=64), bc(ident[0:20, 4:20].unsqueeze(2), [20, 16, 64]))
            v.wait_ge(ss_st.sem, ss_st.at(l, 16 * 8))
            v.nop(nofuse=True)
            v.drain().then_inc(hn_go.sem, 1)
            headnorm(l, 2)
            v.drain().then_inc(fx_r.sem, 1)
            tt(VCs, VCs, ZCs, ALU.mult)
            v.drain().then_inc(oc_r.sem, 1)

            def fox_max(j):
                v.wait_ge(fs_mm.sem, fs_mm.at(l, j + 1))
                v.nop(nofuse=True)
                N = (j // HB + 1) * P
                NV.tensor_reduce(nmx[:, j % 2:j % 2 + 1], PS[:, j % 2, 0:N], AX.X, ALU.max, negate=True).then_inc(fs_nm.sem, 1)

            fox_max(0)
            for j in range(4 * HB):
                i, h = j // HB, j % HB
                v.wait_ge(fp_mm.sem, fp_mm.at(l, j + 1))
                v.nop(nofuse=True)
                if j >= 2:
                    v.wait_ge(fo_mm.sem, fo_mm.at(l, j - 1))
                    v.nop(nofuse=True)
                cp(W[7 + j % 2][:, 0:(i + 1) * P], PS[:, 2 + j % 2, 0:(i + 1) * P]).then_inc(fp_cp.sem, 1)
                if h == HB - 1:
                    v.wait_ge(fo_mm.sem, fo_mm.at(l, j + 1))
                    v.nop(nofuse=True)
                    if i:
                        v.wait_ge(ft_mm.sem, ft_mm.at(l, i))
                        v.nop(nofuse=True)
                    NV.reciprocal(rs8[:, i % 2, :], rs8[:, i % 2, :])
                    v.drain()
                    tt(W[10].rearrange("p (h d) -> p h d", h=HB), PS[:, 4 + i % 2, :].rearrange("p (h d) -> p h d", h=HB),
                       bc(rs8[:, i % 2, :].unsqueeze(2), [P, HB, 64]), ALU.mult).then_inc(fn_r.sem, 1)
                if j + 1 < 4 * HB:
                    fox_max(j + 1)
            QBD = wide(2, 1024).rearrange("p (q c m) -> p q c m", q=NSEQ, c=4)
            NV.memset(wide(2, 1024), 0.0)
            v.drain()
            for h in range(HB):
                hp = slice(64 * (h % 2), 64 * (h % 2) + 64)
                cp(QBD[hp, :, h // 2, 4 * h:4 * h + 4], QBs[hp, h // 2, TP:T].rearrange("p (q t) -> p q t", t=TS))
            v.wait_ge(lg_ld.sem, lg_ld.at(l, 16 * 64))
            v.nop(nofuse=True)
            v.wait_ge(ln_ld.sem, ln_ld.at(l, 16 * 8))
            v.nop(nofuse=True)
            NV.tensor_tensor_scan(LG[0:64, 0:PAST + TS], bc(ones[0:64, 0:1], [64, PAST + TS]), LG[0:64, 0:PAST + TS], 0.0, ALU.mult, ALU.add)
            v.drain().then_inc(lg_r.sem, 1)

            def seq_max(q):
                v.wait_ge(qs_mm.sem, qs_mm.at(l, q + 1))
                v.nop(nofuse=True)
                NV.tensor_reduce(nmx[0:32, q % 2:q % 2 + 1], PS[0:32, 0:3, :].rearrange("p a b -> p (a b)")[:, 0:PAST + TSA], AX.X, ALU.max, negate=True).then_inc(qs_nm.sem, 1)

            seq_max(0)
            for q in range(NSEQ):
                v.wait_ge(qp_mm.sem, qp_mm.at(l, q + 1))
                v.nop(nofuse=True)
                cp(W[1][:, 0:256], PS[:, 3, 0:256])
                cp(W[1][0:32, 256:288], PS[0:32, 3, 256:288])
                v.drain().then_inc(qp_cp.sem, 1)
                NV.reciprocal(rs8[0:32, q % 2, 0:1], rs8[0:32, q % 2, 0:1])
                if q + 1 < NSEQ:
                    seq_max(q + 1)
                v.wait_ge(qo_mm.sem, qo_mm.at(l, q + 1))
                v.nop(nofuse=True)
                if q:
                    v.wait_ge(qt_mm.sem, qt_mm.at(l, q))
                    v.nop(nofuse=True)
                v.drain()
                stt(W[0][0:32, :].rearrange("p (h d) -> p h d", h=HB), PS[0:32, 4, :].rearrange("p (h d) -> p h d", h=HB),
                    rs8[0:32, q % 2, 0:1], bc(cn("md")[0:32, :].unsqueeze(2), [32, HB, 64]), ALU.mult, ALU.mult).then_inc(qn_r.sem, 1)
            v.drain().then_inc(ob_r.sem, 1)
            with v.Fori(0, 2) as kc:
                for c4 in range(4):
                    for st in range(3):
                        m = 3 * c4 + st
                        if st:
                            v.drain()
                        v.wait_ge(mg_sg.sem, mg_sg.at(l, kc * 12 + (m + 1)))
                        ys = 5 * c4 + (1, 1, 4)[st]
                        if st == 0:
                            v.wait_ge(mg_mm.sem, mg_mm.at(l, kc * 4 + (c4 + 1)))
                        else:
                            v.wait_ge(ring_used[ys % 4], tiles_used(l, kc * 5 + (B_MG + ys // 4)))
                        ps = pair(4 * (m % 2) + 2)
                        if st == 0:
                            tt(halves(ZALL[:, kc * 4 + (S_MG + c4), :]), halves(SQ[m % 2]), ps, ALU.mult).then_inc(mg_v.sem, 1)
                        else:
                            tt(halves(SQ[2]), halves(SQ[m % 2]), ps, ALU.mult)
                            v.drain()
                            dst = ZALL[:, kc * 4 + (S_MG + c4), :]
                            tt(dst, dst, SQ[2], ALU.add).then_inc(mg_v.sem, 1)
            v.drain()
            with v.Fori(0, 2) as k:
                for s in range(RING):
                    v.wait_ge(ring_used[s], tiles_used(l, k + B_OUT))
                    ps = pair(2 * (s % 2))
                    residual(k * 4 + s, k * 4 + (16 + s), (0, HT), ps[:, 0, :])
                    residual(k * 4 + s, k * 4 + (16 + s), (HT, HT), ps[:, 1, :])
                    v.drain().then_inc(wo_v.sem, 1)
            norm(l, 1, 24, 32)
            SC = AR[:, S_SC * T:S_SC * T + 2048].rearrange("p (j n) -> p j n", j=16)
            S2 = AR[:, 28 * T:28 * T + 2048].rearrange("p (j n) -> p j n", j=16)
            CD = AR[:, S_CD * T:S_CD * T + 2048].rearrange("p (h a b) -> p h a b", h=8, a=16)
            C2 = AR[:, S_CD * T + 2048:S_CD * T + 4096].rearrange("p (h n) -> p h n", h=8)
            CDf = AR[:, S_CD * T:S_CD * T + 2048].rearrange("p (h n) -> p h n", h=8)
            SV = W[3][:, 0:256].rearrange("p (j k) -> p j k", j=16)
            SI = W[3][:, 256:512].rearrange("p (j k) -> p j k", j=16)
            SIf = W[4][:, 0:256].rearrange("p (j k) -> p j k", j=16)
            BV = W[5][:, 0:128].rearrange("p (h k) -> p h k", h=8)
            BP = W[5][:, 128:256].rearrange("p (h k) -> p h k", h=8)
            BA, BB = W[5][:, 256:384], W[5][:, 384:512]
            AF, BF = W[6][:, 0:128], W[6][:, 128:256]
            SM = W[6][:, 256:272]

            def top16(src, tmp, val, idx, n, w):
                for j in range(n):
                    NV.max(val[0:w, j, 0:8], src[0:w, j, :])
                v.drain()
                for j in range(n):
                    NV.max_index(idx[0:w, j, 0:8].bitcast(U32), val[0:w, j, 0:8], src[0:w, j, :])
                    NV.match_replace(tmp[0:w, j, :], val[0:w, j, 0:8], src[0:w, j, :], LOWEST)
                v.drain()
                for j in range(n):
                    NV.max(val[0:w, j, 8:16], tmp[0:w, j, :])
                v.drain()
                for j in range(n):
                    NV.max_index(idx[0:w, j, 8:16].bitcast(U32), val[0:w, j, 8:16], tmp[0:w, j, :])
                v.drain()

            for p in range(5):
                w = NTS[p][1]
                v.wait_ge(sc_s.sem, sc_s.at(l, p + 1))
                v.nop(nofuse=True)
                top16(SC, S2, SV, SI, 16, w)
                sv = SV[0:w].rearrange("p (h two) k -> p h two k", two=2)
                tt(CD[0:w], bc(sv[:, :, 0, :].unsqueeze(3), [w, 8, 16, 16]), bc(sv[:, :, 1, :].unsqueeze(2), [w, 8, 16, 16]), ALU.add)
                cp(SIf[0:w], SI[0:w].bitcast(U32))
                v.drain()
                top16(CDf, C2, BV, BP, 8, w)
                if p:
                    v.wait_ge(rr_mm.sem, rr_mm.at(l, p))
                    v.nop(nofuse=True)
                tt(W[2][0:w, 0:P].rearrange("p (h k) -> p h k", h=8), BV[0:w], bc(BV[0:w, :, 0:1], [w, 8, 16]), ALU.subtract)
                v.drain().then_inc(tk_v.sem, 1)
                bp = W[5][0:w, 128:256].bitcast(U32)
                ts(BA[0:w, :].bitcast(U32), bp, 4, None, ALU.logical_shift_right)
                ts(BB[0:w, :].bitcast(U32), bp, 15, None, ALU.bitwise_and)
                v.drain()
                cp(AF[0:w, :], BA[0:w, :].bitcast(U32))
                cp(BF[0:w, :], BB[0:w, :].bitcast(U32))
                v.drain()
                si = SIf[0:w].rearrange("p (h two) k -> p h two k", two=2)
                for which, pos, dst in ((0, AF, W[0]), (1, BF, W[1])):
                    e2 = AR[0:w, S_CD * T:S_CD * T + 2048].rearrange("p (n a) -> p n a", a=16)
                    e3 = AR[0:w, S_CD * T:S_CD * T + 2048].rearrange("p (h k a) -> p h k a", h=8, k=16)
                    tt(e2, bc(pos[0:w, :].unsqueeze(2), [w, P, 16]), bc(iota16[0:w, :].unsqueeze(1), [w, P, 16]), ALU.is_equal)
                    v.drain()
                    tt(e3, e3, bc(si[:, :, which, :].unsqueeze(2), [w, 8, 16, 16]), ALU.mult)
                    v.drain()
                    NV.tensor_reduce(dst[0:w, 0:P], e2, AX.X, ALU.add)
                    v.drain()
                v.wait_ge(sx_e.sem, sx_e.at(l, p + 1))
                v.nop(nofuse=True)
                g3 = W[2][0:w, 0:P].rearrange("p (h k) -> p h k", h=8)
                NV.tensor_reduce(SM[0:w, 0:8], g3, AX.X, ALU.add)
                v.drain()
                NV.reciprocal(SM[0:w, 8:16], SM[0:w, 0:8])
                v.drain()
                tt(g3, g3, bc(SM[0:w, 8:16].unsqueeze(2), [w, 8, 16]), ALU.mult)
                v.drain().then_inc(rt_v.sem, 1)
            v.wait_ge(rr_s.sem, rr_s.at(l, 5))
            v.nop(nofuse=True)
            for hf in range(2):
                with v.Fori(0, 34) as k:
                    for b in range(2):
                        v.wait_ge(oh_mm.sem, oh_mm.at(l, k * 2 + (hf * 68 + b - 1)))
                        for j in range(4):
                            t_ = (k * 2 + b) * 4 + (hf * HT + j)
                            if j >= JS:
                                ts(OHJ[b][:, j, :], iota[:, :], RO[:, 1, bass.ds(t_, 1)], None, ALU.is_equal)
                            i = ts(OHI[b][:, j, :], iota[:, :], RO[:, 0, bass.ds(t_, 1)], RO[:, 2, bass.ds(t_, 1)], ALU.is_equal, ALU.mult)
                        i.then_inc(oi_v.sem, 1)
                v.wait_ge(w_ev.sem, w_ev.at(l, (hf + 1) * 68))
                v.nop(nofuse=True)
                with v.Fori(0, G_U) as k:
                    for s in range(RING):
                        v.wait_ge(gl_s.sem, gl_s.at(l, k * 4 + (hf * 128 + s + 1)))
                        row = WB[:, k * 4 + s, :]
                        tt(row, row, GB[s % 2], ALU.mult).then_inc(a_v.sem, 1)
                with v.Fori(0, 4) as d:
                    for b in range(2):
                        v.wait_ge(ring_used[RING - 1], tiles_used(l, d * 8 + (b * 4 + 3 + G_W + hf * (G_U + G_V) + G_U)))
                        residual(d * 2 + b, d * 2 + (40 + b), (hf * HT, HT), PS[:, 6 + b, 0:HT])
                        v.drain().then_inc(y_v.sem, 1)

    @block.scalar
    def _(s_):
        act = nc.scalar.activation
        copy = lambda out, in_: act(out, in_, ACT.Copy)

        s_.wait_ge(init_v, 1)
        act(LB[:, :, :], LB[:, :, :], ACT.Exp)
        act(cT[:, :, :], cT[:, :, :], ACT.Silu)
        s_.drain().then_inc(init_c, 1)
        for g_ in (z_ev, qj_s, w_ev, gl_s):
            s_.drain().then_inc(g_.sem, g_.first)

        def norm(l, n):
            act(XSQ, xT[:, :, :], ACT.Square).then_inc(sq_r.sem, 1)
            s_.wait_ge(ms_mm.sem, ms_mm.at(l, n + 1))
            act(halves(SQ[0]), pair(4), ACT.Sqrt, bias=epsc[:, 0:1], scale=1.0 / DM).then_inc(rt_r.sem, 1)

        def headnorm(l, g, bias):
            base, R = HN_BASE[g], HN_ROWS[g]
            for n, (slot, _, _, _, _) in enumerate(HN[g]):
                if n >= 2:
                    s_.wait_ge(hn_mm.sem, hn_mm.at(l, base + n - 1))
                act(SQ[n % 2], ZALL[:, slot, :], ACT.Square).then_inc(hn_sq.sem, 1)
            s_.wait_ge(hn_mm.sem, hn_mm.at(l, base + len(HN[g])))
            act(halves(SQ[3][0:R, :]), PS[0:R, 4:6, 0:HT], ACT.Sqrt, bias=bias[0:R, :], scale=HN_SCALE[g]).then_inc(hn_rt.sem, 1)

        with s_.Fori(0, L) as l:
            s_.wait_ge(y_v.sem, y_v.at(l, 0))
            norm(l, 0)
            s_.wait_ge(zs_mm.sem, zs_mm.at(l, 1))
            copy(halves(ZS), PS[0:16, 6:8, 0:HT]).then_inc(zs_r.sem, 1)
            for n in range(4):
                s_.wait_ge(ring_used[n], tiles_used(l, B_Z))
                act(halves(Fs[:, n, :]), pair(2 * (n % 2)), ACT.Sigmoid)
                act(halves(Ks[:, n, :]), pair(2 * (n % 2)), ACT.Sigmoid, scale=-1.0).then_inc(z_ev.sem, 1)
            with s_.Fori(0, 3) as k:
                for b in range(4):
                    s_.wait_ge(ring_used[b], tiles_used(l, k + (B_Z + 1)))
                    act(halves(ZALL[:, k * 4 + (S_Q + b), :]), pair(2 * (b % 2)), ACT.Silu).then_inc(z_ev.sem, 1)
            with s_.Fori(0, 7) as k:
                for b in range(4):
                    s_.wait_ge(ring_used[b], tiles_used(l, k + (B_Z + 4)))
                    copy(halves(ZALL[:, k * 4 + (S_I + b), :]), pair(2 * (b % 2))).then_inc(z_ev.sem, 1)
            for p in range(5):
                w = NTS[p][1]
                s_.wait_ge(hv_mm.sem, hv_mm.at(l, p + 1))
                if p >= 2:
                    s_.wait_ge(ho_cp.sem, ho_cp.at(l, p - 1))
                copy(W[5 + p % 2][0:w, :], PS[0:w, 2 * (p % 2), :])
                copy(W[7 + p % 2][0:w, :], PS[0:w, 2 * (p % 2) + 1, :]).then_inc(hv_cp.sem, 1)
            s_.wait_ge(hn_go.sem, hn_go.at(l, 1))
            headnorm(l, 0, epsc[:, 0:1])
            s_.wait_ge(cv_v.sem, cv_v.at(l, 1))
            act(slots(S_QC, 12)[:, :, TP:T], wide(2, 384).rearrange("p (n t) -> p n t", n=12), ACT.Silu).then_inc(cv_s.sem, 1)
            with s_.Fori(0, 6) as k:
                for b in range(2):
                    s_.wait_ge(cv_v.sem, cv_v.at(l, k * 2 + (b + 2)))
                    act(ZALL[:, k * 2 + (S_QC + b), 0:TP], SQ[b][:, 0:TP], ACT.Silu).then_inc(cv_s.sem, 1)
            s_.wait_ge(rw_u.sem, rw_u.at(l, 1))
            act(R_Y, R_Y, ACT.Exp)
            act(RC[0:16, 1:2], pr("al")[0:16, :], ACT.Exp)
            s_.drain()
            act(R_Y, R_Y, ACT.Ln, bias=epsc[0:16, 2:3])
            act(R_B, ZS, ACT.Sigmoid)
            s_.drain().then_inc(rw_e.sem, 1)
            s_.wait_ge(rw_g.sem, rw_g.at(l, 1))
            act(R_E, R_G, ACT.Exp)
            act(R_D, R_D, ACT.Exp)
            s_.drain().then_inc(rw_x.sem, 1)
            headnorm(l, 1, cn("hb2"))
            for p in range(5):
                w = NTS[p][1]
                M0, n4 = p * 18, 4 * w
                bk = lambda b: PS[0:w, b, 0:n4]
                Wn = lambda i: W[i][0:w, 0:n4]
                s_.wait_ge(g_v.sem, g_v.at(l, M0 + 1))
                act(Wn(0), Wn(0), ACT.Exp).then_inc(g_s.sem, 1)
                for m, dst, b in ((3, 5, 3), (4, 7, 4), (5, 5, 6), (6, 6, 1), (8, 10, 4)):
                    s_.wait_ge(g_mm.sem, g_mm.at(l, M0 + m))
                    copy(Wn(dst), bk(b)).then_inc(g_s.sem, 1)
                s_.wait_ge(g_mm.sem, g_mm.at(l, M0 + 16))
                copy(W[1][:, 0:n4], PS[:, 2, 0:n4]).then_inc(g_s.sem, 1)
                if p < NT:
                    s_.wait_ge(g_mm.sem, g_mm.at(l, M0 + 17))
                    copy(W[11][:, :], PS[:, 3, :]).then_inc(g_s.sem, 1)
                else:
                    for h in range(H):
                        s_.wait_ge(gu_mm.sem, gu_mm.at(l, h + 1))
                        copy(W[11][0:32, h * P:(h + 1) * P], PS[0:32, 3, h * P:(h + 1) * P]).then_inc(gu_s.sem, 1)
            s_.wait_ge(hn_go.sem, hn_go.at(l, 2))
            headnorm(l, 2, cn("hb3"))
            for p in range(5):
                w = NTS[p][1]
                s_.wait_ge(fv_mm.sem, fv_mm.at(l, p + 1))
                copy(W[p][0:w, :], PS[0:w, p % 2, :]).then_inc(fv_cp.sem, 1)
            for j in range(4 * HB):
                i, h = j // HB, j % HB
                if h == 0 and i:
                    s_.wait_ge(ft_mm.sem, ft_mm.at(l, i))
                    copy(QBs[:, :, (i - 1) * P:i * P], PS[:, 6, :].rearrange("p (c t) -> p c t", c=4)).then_inc(ft_cp.sem, 1)
                s_.wait_ge(fs_nm.sem, fs_nm.at(l, j + 1))
                if j >= 2:
                    s_.wait_ge(fp_mm.sem, fp_mm.at(l, j - 1))
                act(W[5 + j % 2][:, 0:(i + 1) * P], PS[:, j % 2, 0:(i + 1) * P], ACT.Exp, bias=nmx[:, j % 2:j % 2 + 1],
                    accum_out=rs8[:, i % 2, h:h + 1]).then_inc(fs_ex.sem, 1)
            s_.wait_ge(ft_mm.sem, ft_mm.at(l, 4))
            copy(QBs[:, :, 3 * P:4 * P], PS[:, 6, :].rearrange("p (c t) -> p c t", c=4)).then_inc(ft_cp.sem, 1)

            def seq_exp(q):
                s_.wait_ge(qs_nm.sem, qs_nm.at(l, q + 1))
                act(probs1(q)[0:32, :], PS[0:32, 0:3, :].rearrange("p a b -> p (a b)")[:, 0:PAST + TSA], ACT.Exp,
                    bias=nmx[0:32, q % 2:q % 2 + 1], accum_out=rs8[0:32, q % 2, 0:1]).then_inc(qs_ex.sem, 1)

            def seq_copy(q):
                s_.wait_ge(qt_mm.sem, qt_mm.at(l, q + 1))
                copy(QBs[:, :, TP + q * TS:TP + (q + 1) * TS], PS[:, 5, 0:16].rearrange("p (c t) -> p c t", c=4)).then_inc(qt_cp.sem, 1)

            seq_exp(0)
            for q in range(NSEQ):
                if q + 1 < NSEQ:
                    if q:
                        s_.wait_ge(qn_r.sem, qn_r.at(l, q))
                    seq_exp(q + 1)
                if q:
                    seq_copy(q - 1)
            seq_copy(NSEQ - 1)
            with s_.Fori(0, 2) as kc:
                for m in range(12):
                    gs = 5 * (m // 3) + (0, 2, 3)[m % 3]
                    s_.wait_ge(ring_used[gs % 4], tiles_used(l, kc * 5 + (B_MG + gs // 4)))
                    s_.wait_ge(mg_v.sem, mg_v.at(l, kc * 12 + (m - 1)))
                    act(halves(SQ[m % 2]), pair(4 * (m % 2)), ACT.Sigmoid).then_inc(mg_sg.sem, 1)
            s_.wait_ge(wo_v.sem, wo_v.at(l, 8))
            norm(l, 1)
            with s_.Fori(0, 4) as k:
                for b in range(4):
                    s_.wait_ge(ring_used[b], tiles_used(l, k + B_Q))
                    copy(halves(ZALL[:, k * 4 + (S_QP + b), :]), pair(2 * (b % 2))).then_inc(qj_s.sem, 1)

            def routes(p):
                c0, w = NTS[p]
                s_.wait_ge(rr_mm.sem, rr_mm.at(l, p + 1))
                copy(RO[:, :, c0:c0 + w], PS[:, 4, 0:3 * P].rearrange("p (j t) -> p j t", j=3)[:, :, 0:w]).then_inc(rr_s.sem, 1)

            for p in range(5):
                w = NTS[p][1]
                s_.wait_ge(sc_mm.sem, sc_mm.at(l, p + 1))
                if p:
                    s_.wait_ge(rt_v.sem, rt_v.at(l, p))
                copy(AR[0:w, S_SC * T:S_SC * T + 2048], PS[0:w, 0:4, :].rearrange("p a b -> p (a b)")).then_inc(sc_s.sem, 1)
                if p:
                    routes(p - 1)
                s_.wait_ge(tk_v.sem, tk_v.at(l, p + 1))
                act(W[2][0:w, 0:P], W[2][0:w, 0:P], ACT.Exp).then_inc(sx_e.sem, 1)
            routes(4)
            s_.drain()
            for hf in range(2):
                def columns(b, t0):
                    for j in range(JS):
                        act(OHJ[b][:, j, :], iota[:, :], ACT.Square, bias=RO[:, 1, bass.ds(t0 + j, 1)], scale=-1.0)
                    s_.drain()
                    act(OHJ[b][:, 0:JS, :], OHJ[b][:, 0:JS, :], ACT.Relu, bias=epsc[:, 2:3], scale=-1.0).then_inc(oj_s.sem, 1)

                for b in range(2):
                    columns(b, b * 4 + hf * HT)
                with s_.Fori(0, 33) as k:
                    for b in range(2):
                        s_.wait_ge(oh_mm.sem, oh_mm.at(l, k * 2 + (hf * 68 + b + 1)))
                        copy(WBt[:, bass.ds((k * 2 + b) * 4, 4), :], PS[:, b, :].rearrange("p (t i) -> p t i", t=4)).then_inc(w_ev.sem, 1)
                        columns(b, (k * 2 + b) * 4 + (hf * HT + 8))
                for b in range(2):
                    s_.wait_ge(oh_mm.sem, oh_mm.at(l, hf * 68 + 66 + b + 1))
                    copy(WBt[:, (66 + b) * 4:(67 + b) * 4, :], PS[:, b, :].rearrange("p (t i) -> p t i", t=4)).then_inc(w_ev.sem, 1)
                with s_.Fori(0, G_U) as k:
                    for b in range(4):
                        s_.wait_ge(ring_used[b], tiles_used(l, k + (G_W + hf * (G_U + G_V))))
                        s_.wait_ge(a_v.sem, a_v.at(l, k * 4 + (hf * 128 + b - 1)))
                        act(GB[b % 2], PS[:, 2 + b % 2, 0:HT], ACT.Gelu_apprx_tanh).then_inc(gl_s.sem, 1)

    block_cm.__exit__(None, None, None)


def kernel(**inp):
    import concourse.bacc as bacc
    from concourse.bass_utils import run_bass_kernel_spmd

    A = {k: np.asarray(v) for k, v in inp.items()}
    f32 = np.float32
    C = np.ascontiguousarray

    def fm(x):
        n = x.ndim
        x = x.reshape(x.shape[:-1] + (x.shape[-1] // P, P))
        return np.moveaxis(x, (-1, -2), (n - 2, n - 1))

    xs = np.concatenate([A["x_prompt"].reshape(TP, DM), A["x_sample"].reshape(TSA, DM)], 0)
    cs = np.concatenate([A["c_prompt"], A["c_sample"]], 0)

    def tiles(w):
        n = w.shape[2] // P
        return w.reshape(L, DC, P, n, P).transpose(0, 3, 2, 1, 4)

    w_in = A["w_in"]
    names = ("fa", "qa", "ia", "ga", "qb", "kb", "vb", "fb", "qc", "kc", "vc", "ac", "bc", "zc", "g0", "g1", "g2")
    widths = (512,) * 7 + (HB,) + (512,) * 3 + (H, H) + (512,) + (DM,) * 3
    col, at = {}, 0
    for n_, w_ in zip(names, widths):
        col[n_] = w_in[:, :, at:at + w_]
        at += w_
    zt = tiles(np.concatenate([col[n_] for n_ in ("fa", "qa", "ga", "zc", "ia", "qc", "kc", "vc", "qb", "kb", "vb")], 2))
    gt = [tiles(col[f"g{i}"]) for i in range(3)]
    bt = [A[n_].reshape(L, 4, P, DC, P).transpose(0, 3, 2, 1, 4) for n_ in ("w_br_a", "w_br_b", "w_br_c")]
    ab = np.concatenate([bt[0], bt[1]], 3)
    cc = np.concatenate([bt[2], np.zeros_like(bt[2])], 3)
    mg = np.stack([gt[0], ab, gt[1], gt[2], cc], 2).reshape(L, DC * 5, P, DC, P)
    wst = np.concatenate([tiles(A["w_ada"]), zt, mg, tiles(A["w_out"]), tiles(A["peer_w_q"])], 1)
    wst = C(wst.reshape(L * G_W * RING, P, DC, P))
    u = A["peer_u"].reshape(L, NK, NK, DC, P).transpose(0, 1, 4, 3, 2)
    vv = A["peer_v"].reshape(L, 16, 8, NK, DC, P).transpose(0, 4, 1, 3, 2, 5)
    uv = C(np.concatenate([u, vv.reshape(L, P, P, DC, P)], 1).reshape(L * 256, P, DC, P))
    small = np.concatenate([col["fb"], col["ac"], col["bc"]], 2)
    wsm = C(small.reshape(L, DC, P, 16).transpose(0, 2, 1, 3).reshape(L, P, P))
    prm = np.zeros((L, P, NPR), f32)

    def put(name, x):
        b0, w_ = PR[name]
        prm[:, :x.shape[1], b0:b0 + w_] = x

    put("b_ada", A["b_ada"].reshape(L, 48, P).transpose(0, 2, 1))
    put("nmix", A["norm_mix"].reshape(L, DC, P).transpose(0, 2, 1))
    put("nffn", A["norm_ffn"].reshape(L, DC, P).transpose(0, 2, 1))
    put("hg", A["hgrn_norm"][:, :, None])
    put("qg", np.concatenate([A["fox_q_norm"]] * 2, 1)[:, :, None])
    put("kg", np.concatenate([A["fox_k_norm"]] * 2, 1)[:, :, None])
    put("gg", A["gdn_norm"][:, :, None])
    put("conv", A["gdn_conv_w"].reshape(L, 4, 12, P).transpose(0, 3, 1, 2).reshape(L, P, 48))
    z4 = np.zeros((L, 4), f32)
    put("rb", np.concatenate([A["fox_b_f"], A["gdn_dt_bias"], z4], 1)[:, :, None])
    put("al", np.concatenate([z4, z4, A["gdn_a_log"], z4], 1)[:, :, None])
    put("keys", A["peer_keys"].transpose(0, 3, 1, 2).reshape(L, P, 256))
    npool = A["cache_fox_k"].shape[1]
    ins = {
        "x": C(fm(xs)), "c": C(fm(cs)), "id": np.eye(P, dtype=f32), "ones": np.ones((P, P), f32),
        "iota": C(np.broadcast_to(np.arange(P, dtype=f32), (P, P))), "cn": shape_constants(),
        "lb": C(A["hgrn_lb_logits"].reshape(L, H, P).transpose(2, 0, 1)),
        "pt": C(A["page_table"].reshape(1, 64).astype(np.int32, copy=False)),
        "wst": wst, "uv": uv, "wsm": wsm, "prm": prm,
        "ck": C(A["cache_fox_k"].reshape(L, npool, PAGE, 4, P).transpose(0, 1, 4, 3, 2)),
        "cvv": C(A["cache_fox_v"].reshape(L, npool, PAGE, 512)),
        "cl": C(A["cache_fox_logf"].transpose(0, 1, 3, 2)),
        "hgs": C(A["state_hgrn"].transpose(0, 2, 3, 1, 4).reshape(L, H, P, NSEQ * P)),
        "gds": C(A["state_gdn"].transpose(0, 2, 3, 1, 4).reshape(L, H, P, NSEQ * P)),
        "cvs": C(A["state_gdn_conv"].reshape(L, NSEQ, 3, 12, P).transpose(0, 4, 3, 1, 2).reshape(L, P, 288)),
    }
    outs = {
        "x": (P, DC, T), "fk": (L, P, 4, T), "fv": (L, P, 4, T), "fl": (L, 8, T), "hg_p": (L, P, 512), "gd_p": (L, P, 512),
        "hg_s": (L, H, P, NSEQ * P), "gd_s": (L, H, P, NSEQ * P), "cv": (L, P, 12 * 27),
    }
    nc = bacc.Bacc("TRN2", target_bir_lowering=False, num_devices=1)
    a = {k: nc.dram_tensor(f"in_{k}", v.shape, mybir.dt.from_np(v.dtype), kind="ExternalInput").ap() for k, v in ins.items()}
    o = {k: nc.dram_tensor(f"out_{k}", s, F32, kind="ExternalOutput").ap() for k, s in outs.items()}
    build(nc, a, o)
    r = run_bass_kernel_spmd(nc, [{f"in_{k}": v for k, v in ins.items()}], core_ids=[0]).results[0]
    r = {k: r[f"out_{k}"] for k in outs}

    def rows(x):
        return np.moveaxis(x, -3, -1).swapaxes(-3, -2).reshape(x.shape[:-3] + (x.shape[-1], -1))

    y, fk, fv, fl = rows(r["x"]), rows(r["fk"]), rows(r["fv"]), r["fl"].transpose(0, 2, 1)
    cv = r["cv"].reshape(L, P, 12, 27)
    pr_s = lambda x: x.reshape(L, P, H, P).transpose(0, 2, 1, 3)[:, None]
    sm_s = lambda x: x.reshape(L, H, P, NSEQ, P).transpose(0, 3, 1, 2, 4)
    return tuple(C(z) for z in (
        y[None, :TP], y[TP:].reshape(NSEQ, TS, DM),
        fk[:, None, :TP].reshape(L, 1, TP, HB, 64), fv[:, None, :TP].reshape(L, 1, TP, HB, 64), fl[:, None, :TP],
        pr_s(r["hg_p"]), pr_s(r["gd_p"]), cv[..., 0:3].transpose(0, 3, 2, 1).reshape(L, 1, 3, 1536),
        fk[:, TP:].reshape(L, NSEQ, TS, HB, 64), fv[:, TP:].reshape(L, NSEQ, TS, HB, 64), fl[:, TP:].reshape(L, NSEQ, TS, HB),
        sm_s(r["hg_s"]), sm_s(r["gd_s"]),
        cv[..., 3:].reshape(L, P, 12, NSEQ, 3).transpose(0, 3, 4, 2, 1).reshape(L, NSEQ, 3, 1536)))
```
